# Optimizing a Trainium2 kernel written in Bass

```python
import math
import jax, jax.numpy as jnp
from jax import lax
import numpy as np

D_MODEL = 1024
BATCH = 1
SEQ = 2048
DEPTH = 2

GRID_W = 64
CTX_LEN = 256
N_EVEN = (DEPTH + 1) // 2
N_ODD = DEPTH // 2
EPS = 1e-6
ROPE_BASE = 10000.0

RET_HEADS = 4
RET_DK = 128
RET_DV = 128
RET_QK_W = RET_HEADS * RET_DK
RET_W = RET_HEADS * RET_DV
RET_CHUNK = 128

POOL_GROUPS = 4
POOL_GC = 128
POOL_W = POOL_GROUPS * POOL_GC
POOL_WINDOWS = (2, 4, 8, 16)

EVEN_IN = 2 * RET_QK_W + 2 * RET_W + 2 * POOL_W
EVEN_OUT = RET_W + POOL_W

DIFF_HEADS = 8
DIFF_DH = 64
DIFF_DV = 2 * DIFF_DH
DIFF_QK_W = DIFF_HEADS * 2 * DIFF_DH
DIFF_W = DIFF_HEADS * DIFF_DV
ODD_IN = 2 * DIFF_QK_W + 2 * DIFF_W
Q_BLOCK = 128

kernel_name = "hybrid_retention_pool_diffattn_prefix_dit"

def rmsnorm(x, g):
    xf = x.astype(jnp.float32)
    y = xf * lax.rsqrt(jnp.mean(xf * xf, axis=-1, keepdims=True) + EPS)
    return (y * g.astype(jnp.float32)).astype(x.dtype)

def head_layernorm(x):
    xf = x.astype(jnp.float32)
    mu = jnp.mean(xf, axis=-1, keepdims=True)
    var = jnp.mean(jnp.square(xf - mu), axis=-1, keepdims=True)
    return ((xf - mu) * lax.rsqrt(var + EPS)).astype(x.dtype)

def _rot_half_axis(xa, pos):
    da = xa.shape[-1]
    freqs = ROPE_BASE ** (-jnp.arange(da // 2, dtype=jnp.float32) * 2.0 / da)
    ang = pos[:, None] * freqs[None, :]
    cos = jnp.cos(ang).astype(xa.dtype)
    sin = jnp.sin(ang).astype(xa.dtype)
    x1, x2 = xa[..., : da // 2], xa[..., da // 2:]
    return jnp.concatenate([x1 * cos - x2 * sin, x1 * sin + x2 * cos], axis=-1)

def axial_rope(x, rows, cols):
    half = x.shape[-1] // 2
    return jnp.concatenate([_rot_half_axis(x[..., :half], rows), _rot_half_axis(x[..., half:], cols)], axis=-1)

def to_heads(t, n_heads):
    b, s, _ = t.shape
    return t.reshape(b, s, n_heads, -1).transpose(0, 2, 1, 3)

def from_heads(t):
    b, h, s, d = t.shape
    return t.transpose(0, 2, 1, 3).reshape(b, s, h * d)

def retention_scan(q, k, v, log_g, s0, strict, reverse):
    if reverse:
        q, k, v = jnp.flip(q, axis=2), jnp.flip(k, axis=2), jnp.flip(v, axis=2)
    b, h, t, dk = q.shape
    dv = v.shape[-1]
    n = t // RET_CHUNK
    idx = jnp.arange(RET_CHUNK, dtype=jnp.float32)
    rel = idx[:, None] - idx[None, :]
    mask = (rel > 0) if strict else (rel >= 0)
    lg = log_g.astype(jnp.float32)
    intra = jnp.where(mask[None], jnp.exp(lg[:, None, None] * jnp.where(mask, rel, 0.0)[None]), 0.0).astype(q.dtype)
    q_dec = jnp.exp(lg[:, None] * (idx + 1.0))[..., None].astype(q.dtype)
    k_dec = jnp.exp(lg[:, None] * (RET_CHUNK - 1.0 - idx))[..., None].astype(q.dtype)
    c_dec = jnp.exp(lg * RET_CHUNK)[:, None, None].astype(q.dtype)

    def chunks(a):
        return jnp.moveaxis(a.reshape(b, h, n, RET_CHUNK, a.shape[-1]), 2, 0)

    def step(s, inp):
        qc, kc, vc = inp
        sc = jnp.einsum('bhid,bhjd->bhij', qc, kc) * intra
        o = jnp.einsum('bhij,bhjv->bhiv', sc, vc) + jnp.einsum('bhid,bhdv->bhiv', qc * q_dec, s)
        s = s * c_dec + jnp.einsum('bhjd,bhjv->bhdv', kc * k_dec, vc)
        return s, o

    s, o = lax.scan(step, s0, (chunks(q), chunks(k), chunks(v)))
    o = jnp.moveaxis(o, 0, 2).reshape(b, h, t, dv)
    if reverse:
        o = jnp.flip(o, axis=2)
    return o, s

def pool_mix(p, pool_w, pool_scale):
    b, t, _ = p.shape
    csum = jnp.concatenate([jnp.zeros((b, 1, POOL_W), jnp.float32), jnp.cumsum(p.astype(jnp.float32), axis=1)], axis=1)
    pos = jnp.arange(t)
    outs = []
    for g, win in enumerate(POOL_WINDOWS):
        lo = jnp.maximum(pos - win // 2, 0)
        hi = jnp.minimum(pos + win - win // 2 - 1, t - 1)
        cg = csum[..., g * POOL_GC:(g + 1) * POOL_GC]
        mean = (cg[:, hi + 1] - cg[:, lo]) / (hi - lo + 1).astype(jnp.float32)[None, :, None]
        outs.append(mean.astype(p.dtype) - p[..., g * POOL_GC:(g + 1) * POOL_GC])
    d = jnp.stack(outs, axis=2)
    y = jnp.einsum('btgc,gcd->btgd', d, pool_w).reshape(b, t, POOL_W)
    return y * pool_scale

def even_mixer(h, hc, w_in, w_out, decay_logit, pool_w, pool_scale, rows, cols, ctx_out):
    cut = [RET_QK_W, 2 * RET_QK_W, 2 * RET_QK_W + RET_W, 2 * RET_QK_W + 2 * RET_W, 2 * RET_QK_W + 2 * RET_W + POOL_W]
    q, k, v, g_r, p, g_p = jnp.split(h @ w_in, cut, axis=-1)
    qc, kc, vc, g_rc, pc, g_pc = jnp.split(hc @ w_in, cut, axis=-1)
    kscale = RET_DK ** -0.5
    q = axial_rope(to_heads(q, RET_HEADS), rows, cols)
    k = axial_rope(to_heads(k, RET_HEADS), rows, cols) * kscale
    v = to_heads(v, RET_HEADS)
    qc, kc, vc = to_heads(qc, RET_HEADS), to_heads(kc, RET_HEADS) * kscale, to_heads(vc, RET_HEADS)
    log_g = -jnp.exp(decay_logit.astype(jnp.float32))
    b = h.shape[0]
    s_zero = jnp.zeros((b, RET_HEADS, RET_DK, RET_DV), q.dtype)
    oc_f, sc_f = retention_scan(qc, kc, vc, log_g[0], s_zero, False, False)
    oc_b, sc_b = retention_scan(qc, kc, vc, log_g[1], s_zero, True, True)
    o_f, _ = retention_scan(q, k, v, log_g[0], sc_f, False, False)
    o_b, _ = retention_scan(q, k, v, log_g[1], sc_b, True, True)
    ret = from_heads(head_layernorm(o_f + o_b)) * jax.nn.silu(g_r)
    pool = pool_mix(p, pool_w, pool_scale) * jax.nn.silu(g_p)
    y = jnp.concatenate([ret, pool], axis=-1) @ w_out
    if not ctx_out:
        return y, None
    ret_c = from_heads(head_layernorm(oc_f + oc_b)) * jax.nn.silu(g_rc)
    pool_c = pool_mix(pc, pool_w, pool_scale) * jax.nn.silu(g_pc)
    yc = jnp.concatenate([ret_c, pool_c], axis=-1) @ w_out
    return y, yc

def diff_attend(q, k, v, lam):
    s = jnp.einsum('bhmqd,bhmkd->bhmqk', q, k).astype(jnp.float32) * (DIFF_DH ** -0.5)
    p = jax.nn.softmax(s, axis=-1)
    a = (p[:, :, 0] - lam * p[:, :, 1]).astype(v.dtype)
    return jnp.einsum('bhqk,bhkv->bhqv', a, v)

def diff_attend_blocks(q, k, v, lam):
    b, h, m, t, dh = q.shape
    nb = t // Q_BLOCK
    qb = jnp.moveaxis(q.reshape(b, h, m, nb, Q_BLOCK, dh), 3, 0)
    o = lax.map(lambda qi: diff_attend(qi, k, v, lam), qb)
    return jnp.moveaxis(o, 0, 2).reshape(b, h, t, v.shape[-1])

def odd_mixer(h, hc, w_in, w_out, lam_p, subln, layer_idx, rows, cols, ctx_out):
    cut = [DIFF_QK_W, 2 * DIFF_QK_W, 2 * DIFF_QK_W + DIFF_W]
    q, k, v, g = jnp.split(h @ w_in, cut, axis=-1)
    qc, kc, vc, gc = jnp.split(hc @ w_in, cut, axis=-1)

    def split_qk(t):
        b, s, _ = t.shape
        return t.reshape(b, s, DIFF_HEADS, 2, DIFF_DH).transpose(0, 2, 3, 1, 4)

    q = axial_rope(split_qk(q), rows, cols)
    k = axial_rope(split_qk(k), rows, cols)
    v = to_heads(v, DIFF_HEADS)
    qc, kc, vc = split_qk(qc), split_qk(kc), to_heads(vc, DIFF_HEADS)
    lam_init = 0.8 - 0.6 * math.exp(-0.3 * layer_idx)
    lp = lam_p.astype(jnp.float32)
    lam = jnp.exp(jnp.sum(lp[0] * lp[1])) - jnp.exp(jnp.sum(lp[2] * lp[3])) + lam_init
    k_all = jnp.concatenate([kc, k], axis=3)
    v_all = jnp.concatenate([vc, v], axis=2)
    o = diff_attend_blocks(q, k_all, v_all, lam)
    o = from_heads(rmsnorm(o, subln) * (1.0 - lam_init)) * jax.nn.silu(g)
    y = o @ w_out
    if not ctx_out:
        return y, None
    oc = diff_attend(qc, kc, vc, lam)
    oc = from_heads(rmsnorm(oc, subln) * (1.0 - lam_init)) * jax.nn.silu(gc)
    return y, oc @ w_out

def setup_inputs(seed: int = 0) -> dict:
    key = jax.random.key(seed)
    ks = jax.random.split(key, 18)
    f32 = jnp.float32
    d = D_MODEL
    base_decay = jnp.log(-jnp.log1p(-(2.0 ** (-5.0 - jnp.arange(RET_HEADS, dtype=f32)))))
    return {
        "x": jax.random.normal(ks[0], (BATCH, SEQ, d), f32),
        "c": jax.random.normal(ks[1], (BATCH, d), f32),
        "ctx": jax.random.normal(ks[2], (BATCH, CTX_LEN, d), f32),
        "c_ctx": jax.random.normal(ks[3], (d,), f32),
        "ada_w": jax.random.normal(ks[4], (DEPTH, d, 3 * d), f32) * (0.5 * d ** -0.5),
        "ada_b": jax.random.normal(ks[5], (DEPTH, 3 * d), f32) * 0.01,
        "norm_pre": 1.0 + 0.05 * jax.random.normal(ks[6], (DEPTH, d), f32),
        "norm_post": 1.0 + 0.05 * jax.random.normal(ks[7], (DEPTH, d), f32),
        "ev_w_in": jax.random.normal(ks[8], (N_EVEN, d, EVEN_IN), f32) * d ** -0.5,
        "ev_w_out": jax.random.normal(ks[9], (N_EVEN, EVEN_OUT, d), f32) * EVEN_OUT ** -0.5,
        "ret_decay_logit": base_decay[None, None, :] + 0.05 * jax.random.normal(ks[10], (N_EVEN, 2, RET_HEADS), f32),
        "pool_w": jax.random.normal(ks[11], (N_EVEN, POOL_GROUPS, POOL_GC, POOL_GC), f32) * POOL_GC ** -0.5,
        "pool_scale": 1.0 + 0.1 * jax.random.normal(ks[12], (N_EVEN, POOL_W), f32),
        "od_w_in": jax.random.normal(ks[13], (N_ODD, d, ODD_IN), f32) * d ** -0.5,
        "od_w_out": jax.random.normal(ks[14], (N_ODD, DIFF_W, d), f32) * DIFF_W ** -0.5,
        "diff_lambda": 0.1 * jax.random.normal(ks[15], (N_ODD, 4, DIFF_DH), f32),
        "diff_subln": 1.0 + 0.05 * jax.random.normal(ks[16], (N_ODD, DIFF_DV), f32),
    }

def reference(x, c, ctx, c_ctx, ada_w, ada_b, norm_pre, norm_post, ev_w_in, ev_w_out, ret_decay_logit,
              pool_w, pool_scale, od_w_in, od_w_out, diff_lambda, diff_subln):
    t = x.shape[1]
    ROWS = t // GRID_W
    rows = jnp.repeat(jnp.arange(ROWS), GRID_W).astype(jnp.float32)
    cols = jnp.tile(jnp.arange(GRID_W), ROWS).astype(jnp.float32)
    xc = ctx
    for l in range(DEPTH):
        ctx_out = l < DEPTH - 1
        mod = jax.nn.silu(c) @ ada_w[l] + ada_b[l]
        shift, scale, gate = jnp.split(mod[:, None, :], 3, axis=-1)
        mod_c = jax.nn.silu(c_ctx) @ ada_w[l] + ada_b[l]
        shift_c, scale_c, gate_c = jnp.split(mod_c, 3, axis=-1)
        h = rmsnorm(x, norm_pre[l]) * (1.0 + scale) + shift
        hc = rmsnorm(xc, norm_pre[l]) * (1.0 + scale_c) + shift_c
        i = l // 2
        if l % 2 == 0:
            y, yc = even_mixer(h, hc, ev_w_in[i], ev_w_out[i], ret_decay_logit[i], pool_w[i], pool_scale[i],
                               rows, cols, ctx_out)
        else:
            y, yc = odd_mixer(h, hc, od_w_in[i], od_w_out[i], diff_lambda[i], diff_subln[i], l,
                              rows, cols, ctx_out)
        x = x + gate * rmsnorm(y, norm_post[l])
        if ctx_out:
            xc = xc + gate_c * rmsnorm(yc, norm_post[l])
    return x


_drawn_inputs = setup_inputs


def setup_inputs(seed=0):
    import zlib

    import numpy as np

    out = dict(_drawn_inputs(seed))
    spreads = {}
    factors = {'ada_b': 2.869, 'norm_post': 2.847, 'pool_scale': 3.073, 'diff_subln': 3.677}
    for name, (base, spread) in spreads.items():
        noise = np.random.default_rng([zlib.crc32(name.encode()), seed]).standard_normal(out[name].shape)
        drawn = base * np.exp(spread * noise) if base else spread * noise
        out[name] = __import__('jax').numpy.asarray(drawn.astype(out[name].dtype))
    for name, factor in factors.items():
        out[name] = (out[name] * factor).astype(out[name].dtype)
    return out
```

```python
import math
from contextlib import ExitStack

import numpy as np

import concourse.bass as bass
from concourse import mybir

F32 = mybir.dt.float32
F32R = mybir.dt.float32r
ALU = mybir.AluOpType
ACT = mybir.ActivationFunctionType
AX = mybir.AxisListType.X

P = 128
D = 1024
KC = D // P
SEQ, CTX = 2048, 256
T = SEQ + CTX
NT, CT, LT = T // P, CTX // P, SEQ // P
EPS = 1e-6
GRID_W = 64
ROPE_BASE = 10000.0
RH = 4
PG = 4
POOL_WINDOWS = (2, 4, 8, 16)
HALO = 16
DH = 64
AH = 8
LAM_INIT = 0.8 - 0.6 * math.exp(-0.3 * 1)
KSCALE = float(P) ** -0.5
ASCALE = float(DH) ** -0.5
MID_PAD = 1700
HB = 512

PASSES = [
    dict(name="qk0", tiles=(0, NT), src="norm", layer=0, post="rope", rope=0),
    dict(name="vg0", tiles=(0, NT), src="load", layer=0, post="gate"),
    dict(name="pg0", tiles=(0, NT), src="load", layer=0, post="gate"),
    dict(name="out0", tiles=(0, NT), src="load", layer=0, post="residual"),
    dict(name="k1", tiles=(0, NT), src="norm", layer=1, post="rope", rope=1),
    dict(name="v1", tiles=(0, NT), src="load", layer=1, post="copy"),
    dict(name="q1", tiles=(CT, LT), src="load", layer=1, post="rope", rope=1),
    dict(name="g1", tiles=(CT, LT), src="load", layer=1, post="silu"),
    dict(name="out1", tiles=(CT, LT), src="load", layer=1, post="residual"),
]
NP_ = len(PASSES)


def tiles_before(p, want=lambda q: True):
    return sum(q["tiles"][1] for q in PASSES[:p] if want(q))


def host_constants():
    rows = np.repeat(np.arange(SEQ // GRID_W), GRID_W).astype(np.float32)
    cols = np.tile(np.arange(GRID_W), SEQ // GRID_W).astype(np.float32)

    def rope(head):
        quarter = head // 4
        da = head // 2
        freqs = np.float32(ROPE_BASE) ** (-np.arange(quarter, dtype=np.float32) * np.float32(2.0) / np.float32(da))
        c = np.ones((T, 2, 2, quarter), np.float32)
        s = np.zeros((T, 2, 2, quarter), np.float32)
        for a, pos in enumerate((rows, cols)):
            ang = pos[:, None] * freqs[None, :]
            c[CTX:, a, :, :] = np.cos(ang)[:, None, :]
            s[CTX:, a, 0, :] = -np.sin(ang)
            s[CTX:, a, 1, :] = np.sin(ang)
        return np.stack([c.reshape(T, head), s.reshape(T, head)], 1).reshape(NT, P, 2 * head)

    j, i = np.meshgrid(np.arange(P, dtype=np.float32), np.arange(P, dtype=np.float32), indexing="ij")
    rel = np.stack([np.maximum(i - j, 0), np.maximum(j - i, 0),
                    KSCALE * (i >= j), KSCALE * (j > i)], 1).astype(np.float32)
    t = np.arange(P, dtype=np.float32)
    dec_rows = np.broadcast_to(np.stack([t + 1, P - t]), (P, 2, P)).astype(np.float32)
    dec_cols = np.stack([P - 1 - t, t], 1).astype(np.float32)
    own = np.zeros((P, 3, PG, P), np.float32)
    halo = np.zeros((2 * HALO, 3, PG, P), np.float32)
    for v in range(3):
        for g, win in enumerate(POOL_WINDOWS):
            for t in range(P):
                lo, hi = t - win // 2, t + win // 2 - 1
                if v == 1:
                    lo = max(lo, 0)
                if v == 2:
                    hi = min(hi, P - 1)
                w = np.float32(1.0) / np.float32(hi - lo + 1)
                for s in range(lo, hi + 1):
                    if s < 0:
                        halo[HALO + s, v, g, t] = w
                    elif s >= P:
                        halo[HALO + s - P, v, g, t] = w
                    else:
                        own[s, v, g, t] = w
                own[t, v, g, t] -= 1.0
    return {
        "ident": np.eye(P, dtype=np.float32), "rope0": rope(P), "rope1": rope(DH), "rel": rel.astype(np.float32),
        "dec_rows": np.ascontiguousarray(dec_rows), "dec_cols": dec_cols, "pool_own": own, "pool_halo": halo,
    }


def row_broadcast(row):
    return row.partition_broadcast(P)


def build(nc, A, out):
    def dram(name, shape):
        return nc.dram_tensor(name, shape, F32, kind="Internal").ap()

    hT = [dram("hT0", (NT, P, KC, P)), dram("hT1", (NT, P, KC, P))]
    qk0 = dram("qk0", (NT, P, D))
    vg0 = dram("vg0", (NT, P, D))
    pg0 = dram("pg0", (T, D))
    mixT = dram("mixT", (NT, P, KC, P))
    x1 = dram("x1", (T, D))
    kT1 = dram("kT1", (AH, P, T))
    qT1 = dram("qT1", (AH, P, SEQ))
    v1 = dram("v1", (AH, P, NT, P))
    g1 = dram("g1", (SEQ, D))
    oT1 = dram("oT1", (AH, P, SEQ))

    w_in = [A["ev_w_in"], A["ev_w_in"], A["ev_w_in"], A["ev_w_out"],
            A["od_w_in"], A["od_w_in"], A["od_w_in"], A["od_w_in"], A["od_w_out"]]
    w_col = [0, 1, 2, 0, 1, 2, 0, 3, 0]

    def weight_chunk(p, k):
        return w_in[p][0].rearrange("(k c) (m n) -> k c m n", c=P, n=D)[k, :, w_col[p], :]

    ctx = ExitStack()

    def sb(name, shape, dt=F32, at=ctx):
        return at.enter_context(nc.sbuf_tensor(name, shape, dt))

    def sem(name):
        return ctx.enter_context(nc.semaphore(name))

    with ctx:
        ident = sb("ident_s", [P, P])
        cond = sb("cond_s", [P, KC, 2])
        cond_silu = sb("cond_silu", [P, KC, 2])
        npre = sb("npre_s", [P, 2, KC])
        adab = sb("adab_s", [P, 2, 3 * KC])
        shift = sb("shift", [P, 2, KC, 2])
        scale = sb("scale", [P, 2, KC, 2])
        gate_post = sb("gate_post", [P, 3, D])
        lam_in = sb("lam_in", [P, 4, DH])
        lam_prod = sb("lam_prod", [P, DH])
        lam_sum = sb("lam_sum", [P, 2])
        lam_exp = sb("lam_exp", [P, 2])
        neg_lam = sb("neg_lam", [P, 2])
        subln = sb("subln_s", [P, 2, P])
        minus_half = sb("minus_half", [P, RH])
        eps_col = sb("eps_col", [P, RH])
        zero_col = sb("zero_col", [P, 1])
        minus_one = sb("minus_one", [P, 2])
        ss = sb("ss", [P, 2, 1])
        ms = sb("ms", [P, 2, 1])
        rstd = sb("rstd", [P, 2, 1])
        ss2 = sb("ss2", [P, 2, 1])
        ms2 = sb("ms2", [P, 2, 1])
        rstd2 = sb("rstd2", [P, 2, 1])

        set1 = ExitStack()
        ctx.enter_context(set1)
        setup_bufs = ExitStack()
        ada = sb("ada", [P, 3, 3 * D], at=setup_bufs)
        cond_wide = sb("cond_wide", [P, KC, 2, P], at=setup_bufs)
        adab_row = sb("adab_row", [P, D], at=setup_bufs)
        npost_row = sb("npost_row", [P, D], at=setup_bufs)
        setup_bufs.close()
        whi = [None, None]
        wlo = [None, None]
        whi[1] = sb("whi1", [P, KC, D], F32R, set1)
        wlo[1] = sb("wlo1", [P, KC, D], F32R, set1)
        mid = ExitStack()
        w_raw = sb("w_raw", [P, D], at=mid)
        a_raw = sb("a_raw", [P, 2, KC, P], at=mid)
        a_hi = [sb(f"a_hi{j}", [P, KC, P], F32R, mid) for j in range(2)]
        a_lo = [sb(f"a_lo{j}", [P, KC, P], F32R, mid) for j in range(2)]
        x_in = sb("x_in_s", [P, 2, D], at=mid)
        x_n = sb("x_n", [P, D], at=mid)
        x_sq = sb("x_sq", [P, D], at=mid)
        rope_in = sb("rope_in", [P, 2, 2 * P], at=mid)
        t_cos = sb("t_cos", [P, D], at=mid)
        t_sin = sb("t_sin", [P, D], at=mid)
        y_out = sb("y_out", [P, 2, D], at=mid)
        yT = sb("yT", [P, KC, P], at=mid)
        sb("pad", [P, MID_PAD], at=mid)
        set0 = ExitStack()
        whi[0] = sb("whi0", [P, KC, D], F32R, set0)
        wlo[0] = sb("wlo0", [P, KC, D], F32R, set0)
        set0.close()
        mid_end = nc.sbuf_bytes_remaining
        mid.close()

        ret = ExitStack()
        rel = sb("rel_s", [P, 4, P], at=ret)
        dec_rows = sb("dec_rows_s", [P, 2, P], at=ret)
        dec_cols = sb("dec_cols_s", [P, 2], at=ret)
        log_g = sb("log_g", [P, 2, RH], at=ret)
        log_e = sb("log_e", [P, 2, RH], at=ret)
        e_rel = sb("e_rel", [P, 2, RH, P], at=ret)
        decay_mask = sb("decay_mask", [P, RH, P], at=ret)
        mask_b = sb("mask_b", [P, RH, P], at=ret)
        q_dec = sb("q_dec", [P, 2, RH, P], at=ret)
        k_arg = sb("k_arg", [P, 2, RH], at=ret)
        k_dec = sb("k_dec", [P, 2, RH], at=ret)
        c_dec = sb("c_dec", [P, 2, RH], at=ret)
        pool_own = sb("pool_own_s", [P, 3, PG, P], at=ret)
        pool_halo = sb("pool_halo_s", [2 * HALO, 3, PG, P], at=ret)
        pool_w = sb("pool_w_s", [P, PG, P], at=ret)
        pool_scale = sb("pool_scale_s", [P, PG * P], at=ret)
        back_states = sb("back_states", [P, NT + 1, RH, P], at=ret)
        fwd_state = sb("fwd_state", [P, 2, RH, P], at=ret)
        qk_in = sb("qk_in", [P, 2, D], at=ret)
        vg_in = sb("vg_in", [P, 2, D], at=ret)
        pg_in = sb("pg_in", [P, 2, D], at=ret)
        halo_in = sb("halo_in", [2 * HALO, 2, PG * P], at=ret)
        k_scaled = sb("k_scaled", [P, 2, RH, P], at=ret)
        qkT = sb("qkT", [P, 2, RH, P], at=ret)
        qT_dec = sb("qT_dec", [P, 2, RH, P], at=ret)
        sc_masked = sb("sc_masked", [P, RH, P], at=ret)
        head_sum = sb("head_sum", [P, RH], at=ret)
        head_mean = sb("head_mean", [P, RH], at=ret)
        o_cent = sb("o_cent", [P, RH, P], at=ret)
        o_sq = sb("o_sq", [P, RH, P], at=ret)
        head_var = sb("head_var", [P, RH], at=ret)
        head_var2 = sb("head_var2", [P, RH], at=ret)
        head_rstd = sb("head_rstd", [P, RH], at=ret)
        o_norm = sb("o_norm", [P, RH, P], at=ret)
        mix = sb("mix", [P, KC, P], at=ret)
        gate_scaled = sb("gate_scaled", [P, PG * P], at=ret)
        poolT = sb("poolT", [P, PG, P], at=ret)
        mixT_s = sb("mixT_s", [P, KC, P], at=ret)
        ret.close()
        set1.close()

        att = ExitStack()
        k_hi = sb("k_hi", [P, 2, 2, T], F32R, att)
        k_lo = sb("k_lo", [P, 2, 2, T], F32R, att)
        KS = T // LT
        k_raw = sb("k_raw", [P, 2, 2, KS], at=att)
        v_in = sb("v_in", [P, 2, NT, P], at=att)
        q_raw = sb("q_raw", [P, 2, 2, P], at=att)
        q_st = [sb(f"q_st{j}", [P, 2, P], F32R, att) for j in range(2)]
        prob = sb("prob", [P, 3, T], at=att)
        probT = sb("probT", [P, 3, 4, P], at=att)
        g_in = sb("g_in", [P, 2, P], at=att)
        amax = sb("amax", [P, 2, 3], at=att)
        nbias = sb("nbias", [P, 2, 2], at=att)
        sums = sb("sums", [P, 2, 2, 3], at=att)
        den_part = sb("den_part", [P, 2], at=att)
        denom = sb("denom", [P, 2], at=att)
        lam_den = sb("lam_den", [P, 1], at=att)
        rden = sb("rden", [P, 2, 2], at=att)
        ratio = sb("ratio", [P, 2, 1], at=att)
        o_s = sb("o_s", [P, 2, P], at=att)
        o_sq1 = sb("o_sq1", [P, P], at=att)
        o_ss = sb("o_ss", [P, 2, 1], at=att)
        o_ms = sb("o_ms", [P, 2, 1], at=att)
        o_rstd = sb("o_rstd", [P, 2, 1], at=att)
        o_gated = sb("o_gated", [P, 2, P], at=att)
        oT_s = sb("oT_s", [P, 2, P], at=att)
        assert nc.sbuf_bytes_remaining >= mid_end, "attention runs into weight set 0"
        att.close()

        ps = ctx.enter_context(nc.psum_tensor("ps", [P, 8, HB], F32))
        y_ps = [ps[:, 2 * j:2 * j + 2, :] for j in range(2)]
        tp_ps = [ps[:, 4 + 2 * j:6 + 2 * j, :] for j in range(2)]

        s_const = sem("s_const")
        s_ada = [sem(f"s_ada{j}") for j in range(3)]
        s_ada_used = sem("s_ada_used")
        s_set = sem("s_set")
        s_sete = sem("s_sete")
        s_rows = sem("s_rows")
        s_stage = sem("s_stage")
        s_w_in = sem("s_w_in")
        s_w_hi = sem("s_w_hi")
        s_w_split = sem("s_w_split")
        s_a_in = [sem(f"s_a_in{j}") for j in range(2)]
        s_x_in = [sem(f"s_x_in{j}") for j in range(2)]
        s_rope_in = [sem(f"s_rope_in{j}") for j in range(2)]
        s_ss = sem("s_ss")
        s_ms = sem("s_ms")
        s_rstd = sem("s_rstd")
        s_xn = sem("s_xn")
        s_xT = sem("s_xT")
        s_mo = sem("s_mo")
        s_hi = sem("s_hi")
        s_split = sem("s_split")
        s_mm = sem("s_mm")
        s_tsin = sem("s_tsin")
        s_y = sem("s_y")
        s_y2 = sem("s_y2")
        s_yTp = sem("s_yTp")
        s_yTs = sem("s_yTs")
        s_st = [sem(f"s_st{j}") for j in range(2)]
        s_hst = [sem(f"s_hst{j}") for j in range(2)]
        s_yst = sem("s_yst")
        s_ss2 = sem("s_ss2")
        s_ms2 = sem("s_ms2")
        s_rstd2 = sem("s_rstd2")
        s_res = sem("s_res")

        block = ctx.enter_context(nc.Block())

        def is_norm(q):
            return q["src"] == "norm"

        def is_load(q):
            return q["src"] == "load"

        def is_rope(q):
            return q["post"] == "rope"

        def has_x(q):
            return is_norm(q) or q["post"] == "residual"

        def is_resid(q):
            return q["post"] == "residual"

        def keeps_T(q):
            return is_rope(q) and q["rope"] == 1

        def in_y_out(q):
            return not keeps_T(q)

        def pairs(e, p, body):
            n = PASSES[p]["tiles"][1] // 2
            body(0, True, False)
            with e.Fori(1, n - 1) as i:
                body(i, False, False)
            body(n - 1, False, True)

        def base(p, want=lambda q: True):
            return tiles_before(p, want)

        def stage_end(e, k):
            e.drain().then_inc(s_stage, 1)
            e.wait_ge(s_stage, 5 * k)


        N_CONST = 6

        def sp_setup(e):
            e.dma_start(cond[:, :, :], A["cond"]).then_inc(s_const, 16)
            e.dma_start(ident[:, :], A["ident"]).then_inc(s_const, 16)
            e.dma_start(npre[:, :, :], A["npre"]).then_inc(s_const, 16)
            e.dma_start(adab[:, :, :], A["adab_cols"]).then_inc(s_const, 16)
            e.dma_start(lam_in[:, :, :], row_broadcast(A["diff_lambda"][0])).then_inc(s_const, 16)
            e.dma_start(subln[:, 0, :], row_broadcast(A["diff_subln"][0])).then_inc(s_const, 16)
            for l in range(2):
                if l:
                    e.wait_ge(s_set, 14)
                e.dma_start(adab_row[:, :], row_broadcast(A["ada_b"][l, 2 * D:])).then_inc(s_rows, 16)
                e.dma_start(npost_row[:, :], row_broadcast(A["norm_post"][l])).then_inc(s_rows, 16)
                for k in range(KC):
                    n = KC * l + k
                    if n >= 3:
                        e.wait_ge(s_ada_used, n - 2)
                    e.dma_start(ada[:, n % 3, :], A["ada_w"][l, k * P:(k + 1) * P, :]).then_inc(s_ada[n % 3], 16)
                    if n % 2 == 0:
                        sp_weights(e, 0, n // 2)

        def act_setup(e):
            e.wait_ge(s_const, 16 * N_CONST)
            e.activation(cond_silu[:, :, :], cond[:, :, :], ACT.Silu).then_inc(s_sete, 1)
            e.wait_ge(s_set, 7)
            e.activation(lam_exp[:, :], lam_sum[:, :], ACT.Exp).then_inc(s_sete, 1)

        def pe_setup(e):
            e.wait_ge(s_sete, 1)
            e.wait_ge(s_set, 3)
            for l in range(2):
                for k in range(KC):
                    n = KC * l + k
                    e.wait_ge(s_ada[n % 3], 16 * (n // 3 + 1))
                    w = ada[:, n % 3, :]
                    for b in range(2 * KC):
                        mm = e.matmul(ps[:, l, 2 * b:2 * b + 2], w[:, b * P:(b + 1) * P], cond_silu[:, k, :],
                                      start=(k == 0 and b == 0), stop=(k == KC - 1), skip_group_check=True)
                    for m, stream in enumerate(((0, 1), (1,))[l]):
                        for b in range(2):
                            mm = e.matmul(ps[:, 2 + 4 * l + 2 * m + b, :], cond_wide[:, k, stream, :],
                                          w[:, 2 * D + b * HB:2 * D + (b + 1) * HB], start=(k == 0), stop=(k == KC - 1))
                    mm.then_inc(s_ada_used, 1)

        def dve_setup(e):
            n = 0

            def step(ins):
                nonlocal n
                n += 1
                ins.then_inc(s_set, 1)
                e.wait_ge(s_set, n)

            e.sem_inc(s_split, 2)
            e.sem_inc(s_mm, 2)
            step(e.memset(minus_half[:, :], -0.5))
            step(e.memset(eps_col[:, :], EPS))
            e.wait_ge(s_sete, 1)
            step(e.tensor_copy(cond_wide[:, :, :, :].rearrange("p k s n -> p (k s) n"),
                               cond_silu[:, :, :].rearrange("p k s -> p (k s)").unsqueeze(2)
                               .to_broadcast([P, 2 * KC, P])))
            e.wait_ge(s_const, 16 * N_CONST)
            for m in range(2):
                step(e.tensor_tensor(lam_prod[:, :], lam_in[:, 2 * m, :], lam_in[:, 2 * m + 1, :], ALU.mult))
                step(e.tensor_reduce(lam_sum[:, m:m + 1], lam_prod[:, :], AX.X, ALU.add))
            e.wait_ge(s_sete, 2)
            step(e.tensor_tensor(neg_lam[:, 1:2], lam_exp[:, 1:2], lam_exp[:, 0:1], ALU.subtract))
            step(e.tensor_scalar(neg_lam[:, 0:1], neg_lam[:, 1:2], 1.0, -LAM_INIT, ALU.mult, ALU.add))
            step(e.tensor_scalar(subln[:, 1, :], subln[:, 0, :], 1.0 - LAM_INIT, None, ALU.mult))
            for l in range(2):
                e.wait_ge(s_rows, 32 * (l + 1))
                e.wait_ge(s_ada_used, KC * (l + 1))
                for m in range(2 - l):
                    gate = ps[:, 2 + 4 * l + 2 * m:4 + 4 * l + 2 * m, :].rearrange("p b n -> p (b n)")
                    dst = gate_post[:, 2 * l + m, :]
                    step(e.tensor_tensor(dst, gate, adab_row[:, :], ALU.add))
                    step(e.tensor_tensor(dst, dst, npost_row[:, :], ALU.mult))
                cols = ps[:, l, 0:4 * KC].rearrange("p (h k s) -> p h k s", h=2, k=KC)
                for h, dst in enumerate((shift, scale)):
                    bias = adab[:, l, h * KC:(h + 1) * KC].unsqueeze(2).to_broadcast([P, KC, 2])
                    step(e.tensor_tensor(dst[:, l], cols[:, h], bias, ALU.add))
                step(e.scalar_tensor_tensor(out=scale[:, l], in0=scale[:, l], scalar=1.0,
                                            in1=npre[:, l].unsqueeze(2).to_broadcast([P, KC, 2]),
                                            op0=ALU.add, op1=ALU.mult))
            step(e.memset(zero_col[:, :], 0.0))
            step(e.memset(minus_one[:, :], -1.0))

        def pool_setup(e):
            for k in range(KC):
                pool_weights(e, 0, k)


        def wait_y_out_free(e, p, L, i, j, first):
            prev = PASSES[p] if not first else PASSES[p - 1] if p else None
            if prev is None:
                return
            if keeps_T(prev):
                e.wait_ge(s_yTp, base(p, keeps_T) + (0 if first else L - 1))
            else:
                e.wait_ge(s_st[j], 16 * (base(p, lambda q: not keeps_T(q)) // 2 + (0 if first else i)))

        def act_reads(q):
            return q["post"] in ("gate", "silu")

        def wait_y_ps_free(e, p, L, first):
            prev = PASSES[p] if not first else PASSES[p - 1] if p else None
            if prev is None:
                return
            back = 0 if first else L - 1
            if is_rope(prev):
                e.wait_ge(s_tsin, base(p, is_rope) + back)
            if prev["post"] in ("gate", "copy"):
                e.wait_ge(s_y, base(p) + back)
            if prev["post"] == "silu":
                e.wait_ge(s_y2, base(p, act_reads) + back)
            if is_resid(prev):
                e.wait_ge(s_res, base(p, is_resid) + back)

        def early(p):
            return p < NP_ and is_load(PASSES[p]) and not is_resid(PASSES[p])

        def out_rows(t, h=1):
            return slice(t * P, (t + h) * P)


        def sp_weights(e, p, i):
            if not (isinstance(i, int) and 8 * p + i == 0):
                e.wait_ge(s_w_split, 8 * p + i)
            e.dma_start(w_raw[:, :], weight_chunk(p, i)).then_inc(s_w_in, 16)

        def sp_load(e, p, L, i, j, first):
            q = PASSES[p]
            t0 = q["tiles"][0]
            if is_norm(q):
                if not first:
                    e.wait_ge(s_xn, base(p, is_norm) + L - 1)
                elif base(p, has_x):
                    e.wait_ge(s_y, base(p))
                src = A["x_all"] if q["layer"] == 0 else x1
                e.dma_start(x_in[:, j, :], src.rearrange("(t p) d -> t p d", p=P)[L + t0]).then_inc(s_x_in[j], 16)
                return
            e.wait_ge(s_split, base(p) + L + 1)
            if first and j == 0 and is_norm(PASSES[p - 1]):
                for s in s_hst:
                    e.wait_ge(s, 8 * base(p, is_norm))
            if p == NP_ - 1:
                src = oT1.rearrange("h d (t p) -> t d h p", p=P)[L]
            elif is_resid(q):
                src = mixT[L]
            else:
                src = hT[q["layer"]][L + t0]
            e.dma_start(a_raw[:, j], src).then_inc(s_a_in[j], 16)

        def sp_late(e, p, L, i, j, first):
            q = PASSES[p]
            t0 = q["tiles"][0]
            if is_rope(q):
                w = rope_w(q)
                if not first or base(p, is_rope):
                    e.wait_ge(s_tsin, base(p, is_rope) + (L - 1 if not first else 0))
                e.dma_start(rope_in[:, j, 0:w], A[f"rope{q['rope']}"][L + t0]).then_inc(s_rope_in[j], 16)
            if is_resid(q):
                if not first:
                    e.wait_ge(s_y, base(p) + L - 1)
                else:
                    e.wait_ge(s_xn, base(p, is_norm))
                src = A["x_all"] if q["layer"] == 0 else x1
                e.dma_start(x_in[:, j, :], src.rearrange("(t p) d -> t p d", p=P)[L + t0]).then_inc(s_x_in[j], 16)

        def sp_store_h(e, p, L, j):
            q = PASSES[p]
            e.wait_ge(s_mo, base(p, is_norm) + L + 1)
            e.dma_start(hT[q["layer"]][L], a_raw[:, j]).then_inc(s_hst[j], 16)

        def sp_store(e, p, L, j):
            q = PASSES[p]
            if keeps_T(q):
                dst, t0 = (kT1, 0) if q["name"] == "k1" else (qT1, 0)
                e.wait_ge(s_yTs, base(p, keeps_T) + L + 1)
                e.dma_start(dst.rearrange("h d (t p) -> t d h p", p=P)[L], yT[:, :, :]).then_inc(s_yst, 16)
                return
            e.wait_ge(s_y, base(p) + L + 1)
            y = y_out[:, j, :]
            if q["name"] == "v1":
                e.dma_start(v1.rearrange("h p t d -> t p h d")[L], y.rearrange("p (h d) -> p h d", h=AH))\
                    .then_inc(s_st[j], 16)
                return
            dst = {"qk0": qk0, "vg0": vg0}.get(q["name"])
            if dst is None:
                rows = {"pg0": pg0, "out0": x1, "g1": g1, "out1": out[0]}[q["name"]]
                dst = rows.rearrange("(t p) d -> t p d", p=P)
            e.dma_start(dst[L], y).then_inc(s_st[j], 16)

        def rope_w(q):
            return 2 * P if q["rope"] == 0 else 2 * DH

        def sp_pass(e, p):
            q = PASSES[p]
            nt = q["tiles"][1]
            if q["name"] == "k1":
                for s in s_st:
                    e.wait_ge(s, 8 * base(p, lambda r: not keeps_T(r)))
            if not early(p):
                sp_load(e, p, 0, 0, 0, True)
                sp_load(e, p, 1, 0, 1, True)
            sp_late(e, p, 0, 0, 0, True)
            if is_norm(q):
                sp_store_h(e, p, 0, 0)

            def body(i, first, last):
                for j in range(2):
                    L = 2 * i + j
                    if j == 1 and p + 1 < NP_ and not (last and nt // 2 > KC):
                        sp_weights(e, p + 1, i)
                    if not last:
                        sp_load(e, p, L + 2, i + 1, j, False)
                    if is_norm(q) and not (last and j == 1):
                        sp_store_h(e, p, L + 1, 1 - j)
                    if last and early(p + 1):
                        sp_load(e, p + 1, j, 0, j, True)
                    if not (first and j == 0):
                        sp_store(e, p, L - 1, 1 - j)
                    if not (last and j == 1):
                        sp_late(e, p, L + 1, i, 1 - j, first and j == 0)

            pairs(e, p, body)
            sp_store(e, p, nt - 1, 1)


        def pool_settled(e):
            e.wait_ge(s_stage, 5)

        def pool_weights(e, p, i):
            s = p % 2
            e.wait_ge(s_w_in, 16 * (8 * p + i + 1))
            if p:
                pool_settled(e)
            e.tensor_copy(whi[s][:, i, :], w_raw[:, :]).then_inc(s_w_hi, 1)
            e.wait_ge(s_w_hi, 8 * p + i + 1)
            e.tensor_tensor(wlo[s][:, i, :], w_raw[:, :], whi[s][:, i, :], ALU.subtract)\
                .then_inc(s_w_split, 1)

        def pool_look(e, p, L, j):
            if not is_norm(PASSES[p]):
                return
            nn = base(p, is_norm) + L
            e.wait_ge(s_ss, nn + 1)
            e.tensor_tensor(ms[:, j], ss[:, j], eps_col[:, 0:1], ALU.add).then_inc(s_ms, 1)
            e.wait_ge(s_ms, nn + 1)
            e.tensor_tensor(rstd[:, j], ms[:, j], minus_half[:, 0:1], ALU.pow).then_inc(s_rstd, 1)

        def pool_main(e, p, L, i, j, first):
            q = PASSES[p]
            if first and j == 0 and p and (is_rope(q) or is_resid(q)):
                e.wait_ge(s_y, base(p))
            if is_rope(q):
                wait_y_out_free(e, p, L, i, j, first)
                e.wait_ge(s_tsin, base(p, is_rope) + L + 1)
                e.tensor_tensor(y_out[:, j, :], t_cos[:, :], t_sin[:, :], ALU.add).then_inc(s_y, 1)
            if is_resid(q):
                nr = base(p, is_resid) + L
                e.wait_ge(s_ss2, nr + 1)
                e.tensor_tensor(ms2[:, j], ss2[:, j], eps_col[:, 0:1], ALU.add).then_inc(s_ms2, 1)
                e.wait_ge(s_ms2, nr + 1)
                e.tensor_tensor(rstd2[:, j], ms2[:, j], minus_half[:, 0:1], ALU.pow).then_inc(s_rstd2, 1)
                wait_y_out_free(e, p, L, i, j, first)
                e.wait_ge(s_x_in[j], 16 * (base(p, has_x) // 2 + i + 1))
                e.wait_ge(s_res, nr + 1)
                e.tensor_tensor(y_out[:, j, :], t_sin[:, :], x_in[:, j, :], ALU.add).then_inc(s_y, 1)

        def pool_pass(e, p):
            nt = PASSES[p]["tiles"][1]
            pool_look(e, p, 0, 0)
            pool_look(e, p, 1, 1)
            if p > 0 and p + 1 < NP_:
                e.wait_ge(s_mm, 2 + base(p))

            def body(i, first, last):
                for j in range(2):
                    pool_main(e, p, 2 * i + j, i, j, first)
                    if not last:
                        pool_look(e, p, 2 * i + j + 2, j)
                if p + 1 < NP_ and not (last and nt // 2 > KC):
                    pool_weights(e, p + 1, i)

            pairs(e, p, body)


        def act_square(e, p, i, j):
            e.wait_ge(s_x_in[j], 16 * (base(p, has_x) // 2 + i + 1))
            e.activation(x_sq[:, :], x_in[:, j, :], ACT.Square, scale=D ** -0.5, accum_out=ss[:, j])\
                .then_inc(s_ss, 1)

        def act_look(e, p, L, i, j, more):
            q = PASSES[p]
            if is_norm(q):
                nn = base(p, is_norm) + L
                if not (isinstance(nn, int) and nn == 0):
                    e.wait_ge(s_xT, nn)
                e.wait_ge(s_rstd, nn + 1)
                e.activation(x_n[:, :], x_in[:, j, :], ACT.Identity, scale=rstd[:, j]).then_inc(s_xn, 1)
                if more:
                    act_square(e, p, i + j, 1 - j)
                e.wait_ge(s_mo, nn + 1)
            else:
                e.wait_ge(s_a_in[j], 16 * (base(p, is_load) // 2 + i + 1))
            e.wait_ge(s_mm, base(p) + L + 1)
            e.activation(a_hi[j][:, :, :], a_raw[:, j], ACT.Copy).then_inc(s_hi, 1)

        def act_main(e, p, L, i, j, first):
            q = PASSES[p]
            y = y_ps[j].rearrange("p b n -> p (b n)")
            if keeps_T(q) and not (first and j == 0):
                act_yT(e, p, L - 1)
            if q["post"] == "gate":
                wait_y_out_free(e, p, L, i, j, first)
                e.wait_ge(s_mm, 2 + base(p) + L + 1)
                e.activation(y_out[:, j, HB:], y[:, HB:], ACT.Silu).then_inc(s_y2, 1)
            if q["post"] == "silu":
                e.wait_ge(s_y, base(p) + L)
                e.wait_ge(s_mm, 2 + base(p) + L + 1)
                e.activation(t_cos[:, :], y, ACT.Silu).then_inc(s_y2, 1)
            if is_resid(q):
                e.wait_ge(s_y, base(p) + L)
                e.wait_ge(s_mm, 2 + base(p) + L + 1)
                e.activation(t_cos[:, :], y, ACT.Square, scale=D ** -0.5, accum_out=ss2[:, j]).then_inc(s_ss2, 1)

        def act_yT(e, p, L):
            nT = base(p, keeps_T) + L
            if not (isinstance(nT, int) and nT == 0):
                e.wait_ge(s_yst, 16 * nT)
            e.wait_ge(s_yTp, nT + 1)
            factor = ASCALE if PASSES[p]["name"] == "q1" else 1.0
            e.activation(yT[:, :, :], tp_ps[1].rearrange("p b (k n) -> p (b k) n", n=P), ACT.Copy, scale=factor)\
                .then_inc(s_yTs, 1)

        def act_pass(e, p):
            nt = PASSES[p]["tiles"][1]
            if not early(p):
                if is_norm(PASSES[p]):
                    act_square(e, p, 0, 0)
                act_look(e, p, 0, 0, 0, True)

            def body(i, first, last):
                for j in range(2):
                    L = 2 * i + j
                    if not (last and j == 1):
                        act_look(e, p, L + 1, i + j, 1 - j, not last)
                    elif early(p + 1):
                        act_look(e, p + 1, 0, 0, 0, True)
                    act_main(e, p, L, i, j, first)

            pairs(e, p, body)
            if keeps_T(PASSES[p]):
                act_yT(e, p, nt - 1)


        def dve_look(e, p, L, i, j, stream):
            q = PASSES[p]
            if is_norm(q):
                nn = base(p, is_norm) + L
                l = q["layer"]
                if not (isinstance(nn, int) and nn < 2):
                    e.wait_ge(s_hst[j], 16 * (base(p, is_norm) // 2 + i))
                e.wait_ge(s_xT, nn + 1)
                xT = tp_ps[0].rearrange("p b (k n) -> p (b k) n", n=P)
                for k in range(KC):
                    last = e.tensor_scalar(a_raw[:, j, k, :], xT[:, k, :], scale[:, l, k, stream:stream + 1],
                                           shift[:, l, k, stream:stream + 1], ALU.mult, ALU.add)
                last.then_inc(s_mo, 1)
            e.wait_ge(s_hi, base(p) + L + 1)
            e.tensor_tensor(a_lo[j][:, :, :], a_raw[:, j], a_hi[j][:, :, :], ALU.subtract).then_inc(s_split, 1)

        def dve_main(e, p, L, i, j, first):
            q = PASSES[p]
            if first and j == 0 and q["post"] in ("gate", "copy", "silu"):
                e.wait_ge(s_y, base(p))
            y = y_ps[j].rearrange("p b n -> p (b n)")
            if is_rope(q):
                hd = rope_w(q) // 2
                e.wait_ge(s_rope_in[j], 16 * (base(p, is_rope) // 2 + i + 1))
                if not (isinstance(L, int) and L + base(p) == 0):
                    e.wait_ge(s_y, base(p) + L)
                e.wait_ge(s_mm, 2 + base(p) + L + 1)
                c = rope_in[:, j, 0:hd].unsqueeze(1).to_broadcast([P, D // hd, hd])
                e.tensor_tensor(t_cos.rearrange("p (h d) -> p h d", d=hd), y.rearrange("p (h d) -> p h d", d=hd),
                                c, ALU.mult)
                s = rope_in[:, j, hd:2 * hd].rearrange("p (a b d) -> p a b d", a=2, b=2)
                yv = y.rearrange("p (h a b d) -> p h a b d", a=2, b=2, d=hd // 4)
                tv = t_sin.rearrange("p (h a b d) -> p h a b d", a=2, b=2, d=hd // 4)
                for b in range(2):
                    sv = s[:, :, b, :].unsqueeze(1).to_broadcast([P, D // hd, 2, hd // 4])
                    last = e.tensor_tensor(tv[:, :, :, b, :], yv[:, :, :, 1 - b, :], sv, ALU.mult)
                last.then_inc(s_tsin, 1)
            if q["post"] in ("gate", "copy"):
                w = HB if q["post"] == "gate" else D
                wait_y_out_free(e, p, L, i, j, first)
                if q["post"] == "gate":
                    e.wait_ge(s_y2, base(p, act_reads) + L + 1)
                e.wait_ge(s_mm, 2 + base(p) + L + 1)
                e.tensor_copy(y_out[:, j, 0:w], y[:, 0:w]).then_inc(s_y, 1)
            if q["post"] == "silu":
                wait_y_out_free(e, p, L, i, j, first)
                e.wait_ge(s_y2, base(p, act_reads) + L + 1)
                e.tensor_tensor(y_out[:, j, :].rearrange("p (h d) -> p h d", d=P),
                                t_cos.rearrange("p (h d) -> p h d", d=P),
                                subln[:, 1:2, :].to_broadcast([P, AH, P]), ALU.mult).then_inc(s_y, 1)
            if is_resid(q):
                g = 2 if q["layer"] else 0 if first else 1
                e.wait_ge(s_y, base(p) + L)
                e.wait_ge(s_rstd2, base(p, is_resid) + L + 1)
                e.scalar_tensor_tensor(out=t_sin[:, :], in0=y, scalar=rstd2[:, j], in1=gate_post[:, g, :],
                                       op0=ALU.mult, op1=ALU.mult).then_inc(s_res, 1)

        def dve_pass(e, p):
            ctx_first = PASSES[p]["tiles"][0] == 0
            if not early(p):
                dve_look(e, p, 0, 0, 0, 0)

            def body(i, first, last):
                for j in range(2):
                    L = 2 * i + j
                    if not (last and j == 1):
                        dve_look(e, p, L + 1, i + j, 1 - j, 0 if first and j == 0 else 1)
                    elif early(p + 1):
                        dve_look(e, p + 1, 0, 0, 0, 0)
                    dve_main(e, p, L, i, j, first)

            pairs(e, p, body)


        def pe_xT(e, p, L):
            nn = base(p, is_norm) + L
            if not (isinstance(nn, int) and nn == 0):
                e.wait_ge(s_mo, nn)
            e.wait_ge(s_xn, nn + 1)
            xT = tp_ps[0].rearrange("p b (k n) -> p (b k) n", n=P)
            for k in range(KC):
                last = e.transpose(xT[:, k, :], x_n[:, k * P:(k + 1) * P], ident[:, :])
            last.then_inc(s_xT, 1)

        def pe_yT(e, p, L, j):
            nT = base(p, keeps_T) + L
            if not (isinstance(nT, int) and nT == 0):
                e.wait_ge(s_yTs, nT)
            e.wait_ge(s_y, base(p) + L + 1)
            y = tp_ps[1].rearrange("p b (k n) -> p (b k) n", n=P)
            for k in range(KC):
                last = e.transpose(y[:, k, :], y_out[:, j, k * P:(k + 1) * P], ident[:, :])
            last.then_inc(s_yTp, 1)

        def pe_tile(e, p, L, j, first, last_tile):
            q = PASSES[p]
            wait_y_ps_free(e, p, L, first)
            e.wait_ge(s_split, 2 + base(p) + L + 1)
            hi, lo = whi[p % 2], wlo[p % 2]
            for k in range(KC):
                for a, w in ((a_hi[j], hi), (a_hi[j], lo), (a_lo[j], hi)):
                    for b in range(2):
                        mm = e.matmul(y_ps[j][:, b, :], a[:, k, :], w[:, k, b * HB:(b + 1) * HB],
                                      start=(k == 0 and a is a_hi[j] and w is hi),
                                      stop=(k == KC - 1 and a is a_lo[j]))
                if k == 2 and keeps_T(q) and not (first and j == 0):
                    pe_yT(e, p, L - 1, 1 - j)
                if k == 3 and is_norm(q) and not last_tile:
                    pe_xT(e, p, L + 1)
            mm.then_inc(s_mm, 1)

        def pe_pass(e, p):
            nt = PASSES[p]["tiles"][1]
            if is_norm(PASSES[p]):
                pe_xT(e, p, 0)
            e.wait_ge(s_w_split, 8 * (p + 1))

            def body(i, first, last):
                for j in range(2):
                    pe_tile(e, p, 2 * i + j, j, first, last and j == 1)

            pairs(e, p, body)
            if keeps_T(PASSES[p]):
                pe_yT(e, p, nt - 1, 1)


        s_rc = sem("s_rc")
        s_rv = sem("s_rv")
        s_ra = sem("s_ra")
        s_b_in = [sem(f"s_b_in{j}") for j in range(2)]
        s_b_k = sem("s_b_k")
        s_b_U = sem("s_b_U")
        s_b_S = sem("s_b_S")
        s_f_in = [sem(f"s_f_in{j}") for j in range(2)]
        s_f_T = sem("s_f_T")
        s_f_qkT = sem("s_f_qkT")
        s_f_qd = sem("s_f_qd")
        s_f_dT = sem("s_f_dT")
        s_f_pT = sem("s_f_pT")
        s_f_k = sem("s_f_k")
        s_f_g = sem("s_f_g")
        s_f_U = sem("s_f_U")
        s_f_S = sem("s_f_S")
        s_f_sc = sem("s_f_sc")
        s_f_scm = sem("s_f_scm")
        s_f_yp = sem("s_f_yp")
        s_f_o = sem("s_f_o")
        s_f_sum = sem("s_f_sum")
        s_f_oc = sem("s_f_oc")
        s_f_sq = sem("s_f_sq")
        s_f_var = sem("s_f_var")
        s_f_ve = sem("s_f_ve")
        s_f_rs = sem("s_f_rs")
        s_f_on = sem("s_f_on")
        s_f_mixr = sem("s_f_mixr")
        s_f_mixp = sem("s_f_mixp")
        s_f_fT = sem("s_f_fT")
        s_f_fTs = sem("s_f_fTs")
        s_f_st = sem("s_f_st")

        qkT_ps = ps[:, 0:2, :].rearrange("p a (h n) -> p a h n", n=P)
        sc_ps, o_ps, U_ps, dT_ps, yp_ps, fT_ps = [ps[:, b, :].rearrange("p (h n) -> p h n", n=P) for b in range(2, 8)]
        U_back = [fT_ps, yp_ps]

        def heads(x):
            return x.unsqueeze(2).to_broadcast([P, RH, P])

        def back_runs(e, body):
            for m, (c, s, s_next) in enumerate(((1, NT - 1, NT), (0, NT, NT - 2))):
                body(m, m, c, s, s_next, m == 0)
            with e.Fori(1, NT // 2) as i:
                for j in range(2):
                    body(2 * i + j, j, (-2) * i + (NT + 1 - j), (-2) * i + (NT - j), (-2) * i + (NT - 1 - j), False)

        def chunk_runs(e, body):
            n = NT // 2
            for j, v in ((0, 1), (1, 2)):
                body(j, j, 0, v, j == 0, False)
            for j, v in ((0, 1), (1, 0)):
                body(2 + j, j, 1, v, False, False)
            with e.Fori(2, n - 1) as i:
                for j in range(2):
                    body(2 * i + j, j, i, 0, False, False)
            for j, v in ((0, 0), (1, 2)):
                body(NT - 2 + j, j, n - 1, v, False, j == 1)

        def sp_ret(e):
            e.dma_start(log_g[:, :, :], row_broadcast(A["ret_decay_logit"][0])).then_inc(s_rc, 16)
            e.dma_start(rel[:, :, :], A["rel"]).then_inc(s_rc, 16)
            e.dma_start(dec_rows[:, :, :], A["dec_rows"]).then_inc(s_rc, 16)
            e.dma_start(dec_cols[:, :], A["dec_cols"]).then_inc(s_rc, 16)
            e.dma_start(pool_own[:, :, :, :], A["pool_own"]).then_inc(s_rc, 16)
            e.dma_start(pool_halo[:, :, :, :], A["pool_halo"]).then_inc(s_rc, 16)
            e.dma_start(pool_w[:, :, :], A["pool_w"][0].rearrange("g c d -> c g d")).then_inc(s_rc, 16)
            e.dma_start(pool_scale[:, :], row_broadcast(A["pool_scale"][0])).then_inc(s_rc, 16)

            def back(m, j, c, s, s_next, first):
                if not (isinstance(m, int) and m < 2):
                    e.wait_ge(s_b_U, m - 1)
                e.dma_start(qk_in[:, j, HB:], qk0[c, :, HB:]).then_inc(s_b_in[j], 16)
                e.dma_start(vg_in[:, j, 0:HB], vg0[c, :, 0:HB]).then_inc(s_b_in[j], 16)

            back_runs(e, back)
            blocks = pg0.rearrange("(n r) d -> n r d", r=HALO)
            per = P // HALO

            def load(m, j, i, v, first, last):
                if isinstance(m, int) and m < 2:
                    e.wait_ge(s_b_U, NT)
                else:
                    e.wait_ge(s_f_mixr, m - 1)
                e.dma_start(qk_in[:, j, :], qk0[m]).then_inc(s_f_in[j], 16)
                e.dma_start(vg_in[:, j, :], vg0[m]).then_inc(s_f_in[j], 16)
                e.dma_start(pg_in[:, j, :], pg0.rearrange("(t p) d -> t p d", p=P)[m]).then_inc(s_f_in[j], 16)
                before = 0 if first else per * m - 1
                behind = NT * per - 1 if last else per * m + per
                e.dma_start(halo_in[0:HALO, j, :], blocks[before, :, 0:HB]).then_inc(s_f_in[j], 16)
                e.dma_start(halo_in[HALO:2 * HALO, j, :], blocks[behind, :, 0:HB]).then_inc(s_f_in[j], 16)

            def store(m):
                e.wait_ge(s_f_fTs, 2 * m + 2)
                e.dma_start(mixT[m], mixT_s[:, :, :]).then_inc(s_f_st, 16)

            def body(m, j, i, v, first, last):
                load(m, j, i, v, first, last)
                if not (isinstance(m, int) and m < 2):
                    store(m - 2)

            chunk_runs(e, body)
            store(NT - 2)
            store(NT - 1)
            e.wait_ge(s_f_st, 16 * NT)

        def act_ret(e):
            e.wait_ge(s_rc, 128)
            e.activation(log_e[:, :, :], log_g[:, :, :], ACT.Exp).then_inc(s_ra, 1)
            e.wait_ge(s_rv, 2)
            for d in range(2):
                for h in range(RH):
                    e.activation(e_rel[:, d, h, :], rel[:, d, :], ACT.Exp, scale=log_g[:, d, h:h + 1])
                    e.activation(q_dec[:, d, h, :], dec_rows[:, d, :], ACT.Exp, scale=log_g[:, d, h:h + 1])
            e.activation(c_dec[:, :, :], log_g[:, :, :], ACT.Exp, scale=float(P))
            e.activation(k_dec[:, :, :], k_arg[:, :, :], ACT.Exp).then_inc(s_ra, 1)

            def mix_half(m, half):
                if half == 0 and not (isinstance(m, int) and m == 0):
                    e.wait_ge(s_f_st, 16 * m)
                e.wait_ge(s_f_fT, 2 * m + half + 1)
                e.activation(mixT_s[:, RH * half:RH * half + RH, :], fT_ps, ACT.Copy).then_inc(s_f_fTs, 1)

            def body(m, j, i, v, first, last):
                if not first:
                    e.wait_ge(s_f_sc, m)
                    e.wait_ge(s_f_qd, m)
                e.wait_ge(s_f_T, m + 1)
                e.activation(qkT[:, :, :, :], qkT_ps, ACT.Copy).then_inc(s_f_qkT, 1)
                if not first:
                    mix_half(m - 1, 0)
                    e.wait_ge(s_f_yp, m)
                e.wait_ge(s_f_dT, m + 1)
                e.activation(poolT[:, :, :], dT_ps, ACT.Copy).then_inc(s_f_pT, 1)
                if not first:
                    mix_half(m - 1, 1)
                e.wait_ge(s_f_oc, m + 1)
                e.activation(o_sq[:, :, :], o_cent[:, :, :], ACT.Square, scale=P ** -0.5).then_inc(s_f_sq, 1)

            chunk_runs(e, body)
            mix_half(NT - 1, 0)
            mix_half(NT - 1, 1)

        def dve_ret(e):
            n = 0

            def step(ins):
                nonlocal n
                n += 1
                ins.then_inc(s_rv, 1)
                e.wait_ge(s_rv, n)

            e.wait_ge(s_ra, 1)
            step(e.tensor_scalar(log_g[:, :, :], log_e[:, :, :], -1.0, None, ALU.mult))
            for d in range(2):
                ins = e.tensor_scalar(k_arg[:, d, :], log_g[:, d, :], dec_cols[:, d:d + 1], None, ALU.mult)
            step(ins)
            e.wait_ge(s_ra, 2)
            step(e.tensor_scalar(k_dec[:, :, :], k_dec[:, :, :], KSCALE, None, ALU.mult))
            for d, dst in ((0, decay_mask), (1, mask_b)):
                step(e.tensor_tensor(dst[:, :, :], e_rel[:, d], rel[:, 2 + d:3 + d, :].to_broadcast([P, RH, P]),
                                     ALU.mult))
            step(e.tensor_tensor(decay_mask[:, :, :], decay_mask[:, :, :], mask_b[:, :, :], ALU.add))
            e.memset(back_states[:, NT - 1], 0.0).then_inc(s_b_S, 1)
            e.memset(fwd_state[:, 0], 0.0).then_inc(s_f_S, 1)

            def back(m, j, c, s, s_next, first):
                e.wait_ge(s_b_S, m + 1)
                e.wait_ge(s_b_U, m + 1)
                for h in range(RH):
                    ins = e.scalar_tensor_tensor(out=back_states[:, s_next, h, :], in0=back_states[:, s, h, :],
                                                 scalar=c_dec[:, 1, h:h + 1], in1=U_back[j][:, h, :],
                                                 op0=ALU.mult, op1=ALU.add)
                ins.then_inc(s_b_S, 1)

            back_runs(e, back)

            def body(m, j, i, v, first, last):
                if not first:
                    e.wait_ge(s_f_o, m)
                e.wait_ge(s_f_qkT, m + 1)
                for d in range(2):
                    ins = e.tensor_tensor(qT_dec[:, d], qkT[:, 0], q_dec[:, d], ALU.mult)
                ins.then_inc(s_f_qd, 1)
                e.wait_ge(s_f_sc, m + 1)
                e.tensor_tensor(sc_masked[:, :, :], sc_ps, decay_mask[:, :, :], ALU.mult).then_inc(s_f_scm, 1)
                e.wait_ge(s_f_S, m + 1)
                e.wait_ge(s_f_U, m + 1)
                for h in range(RH):
                    ins = e.scalar_tensor_tensor(out=fwd_state[:, 1 - j, h, :], in0=fwd_state[:, j, h, :],
                                                 scalar=c_dec[:, 0, h:h + 1], in1=U_ps[:, h, :],
                                                 op0=ALU.mult, op1=ALU.add)
                ins.then_inc(s_f_S, 1)
                if not first:
                    e.wait_ge(s_f_fT, 2 * m)
                e.wait_ge(s_f_g, m + 1)
                e.wait_ge(s_f_yp, m + 1)
                e.tensor_tensor(mix[:, RH:, :], yp_ps, gate_scaled.rearrange("p (h n) -> p h n", n=P), ALU.mult)\
                    .then_inc(s_f_mixp, 1)
                e.wait_ge(s_f_o, m + 1)
                e.tensor_reduce(head_sum[:, :], o_ps, AX.X, ALU.add).then_inc(s_f_sum, 1)
                e.wait_ge(s_f_sum, 2 * m + 1)
                e.tensor_scalar(head_mean[:, :], head_sum[:, :], -1.0 / P, None, ALU.mult).then_inc(s_f_sum, 1)
                e.wait_ge(s_f_sum, 2 * m + 2)
                e.tensor_tensor(o_cent[:, :, :], o_ps, heads(head_mean[:, :]), ALU.add).then_inc(s_f_oc, 1)
                e.wait_ge(s_f_sq, m + 1)
                e.tensor_reduce(head_var[:, :], o_sq[:, :, :], AX.X, ALU.add).then_inc(s_f_var, 1)
                e.wait_ge(s_f_rs, m + 1)
                e.tensor_tensor(o_norm[:, :, :], o_cent[:, :, :], heads(head_rstd[:, :]), ALU.mult).then_inc(s_f_on, 1)
                e.wait_ge(s_f_on, m + 1)
                e.tensor_tensor(mix[:, 0:RH, :], o_norm[:, :, :],
                                vg_in[:, j, HB:].rearrange("p (h n) -> p h n", n=P), ALU.mult).then_inc(s_f_mixr, 1)

            chunk_runs(e, body)

        def pool_ret(e):
            e.wait_ge(s_rv, 3)

            def back(m, j, c, s, s_next, first):
                if not (isinstance(m, int) and m < 2):
                    e.wait_ge(s_b_U, m - 1)
                e.wait_ge(s_b_in[j], 32 * (m // 2 + 1) if isinstance(m, int) else 16 * (m - j) + 32)
                e.tensor_tensor(k_scaled[:, j], qk_in[:, j, HB:].rearrange("p (h n) -> p h n", n=P),
                                heads(k_dec[:, 1, :]), ALU.mult).then_inc(s_b_k, 1)

            back_runs(e, back)

            def body(m, j, i, v, first, last):
                if isinstance(m, int) and m < 2:
                    e.wait_ge(s_b_U, NT)
                else:
                    e.wait_ge(s_f_U, m - 1)
                e.wait_ge(s_f_in[j], 80 * (i + 1))
                e.tensor_tensor(k_scaled[:, j], qk_in[:, j, HB:].rearrange("p (h n) -> p h n", n=P),
                                heads(k_dec[:, 0, :]), ALU.mult).then_inc(s_f_k, 1)
                if not first:
                    e.wait_ge(s_f_mixp, m)
                e.tensor_tensor(gate_scaled[:, :], pg_in[:, j, HB:], pool_scale[:, :], ALU.mult).then_inc(s_f_g, 1)
                e.wait_ge(s_f_var, m + 1)
                e.tensor_tensor(head_var2[:, :], head_var[:, :], eps_col[:, :], ALU.add).then_inc(s_f_ve, 1)
                e.wait_ge(s_f_ve, m + 1)
                e.tensor_tensor(head_rstd[:, :], head_var2[:, :], minus_half[:, :], ALU.pow).then_inc(s_f_rs, 1)

            chunk_runs(e, body)

        def pe_ret(e):
            def back(m, j, c, s, s_next, first):
                if not (isinstance(m, int) and m < 2):
                    e.wait_ge(s_b_S, m)
                e.wait_ge(s_b_k, m + 1)
                for h in range(RH):
                    mm = e.matmul(U_back[j][:, h, :], k_scaled[:, j, h, :], vg_in[:, j, h * P:(h + 1) * P],
                                  start=True, stop=True)
                mm.then_inc(s_b_U, 1)

            back_runs(e, back)
            e.wait_ge(s_b_S, NT + 1)

            def mix_half(m, half):
                e.wait_ge(s_f_mixp if half else s_f_mixr, m + 1)
                if not (isinstance(m, int) and m == 0 and half == 0):
                    e.wait_ge(s_f_fTs, 2 * m + half)
                for h in range(RH):
                    t = e.transpose(fT_ps[:, h, :], mix[:, RH * half + h, :], ident[:, :])
                t.then_inc(s_f_fT, 1)

            def body(m, j, i, v, first, last):
                if not first:
                    e.wait_ge(s_f_qkT, m)
                e.wait_ge(s_f_in[j], 80 * (i + 1))
                for a in range(2):
                    for h in range(RH):
                        t = e.transpose(qkT_ps[:, a, h, :], qk_in[:, j, (RH * a + h) * P:(RH * a + h + 1) * P],
                                        ident[:, :])
                t.then_inc(s_f_T, 1)
                if not first:
                    e.wait_ge(s_f_pT, m)
                for g in range(PG):
                    e.matmul(dT_ps[:, g, :], pg_in[:, j, g * P:(g + 1) * P], pool_own[:, v, g, :],
                             start=True, stop=False)
                    mm = e.matmul(dT_ps[:, g, :], halo_in[:, j, g * P:(g + 1) * P], pool_halo[:, v, g, :],
                                  start=False, stop=True)
                mm.then_inc(s_f_dT, 1)
                e.wait_ge(s_f_S, m + 1)
                e.wait_ge(s_f_k, m + 1)
                for h in range(RH):
                    mm = e.matmul(U_ps[:, h, :], k_scaled[:, j, h, :], vg_in[:, j, h * P:(h + 1) * P],
                                  start=True, stop=True)
                mm.then_inc(s_f_U, 1)
                if not first:
                    mix_half(m - 1, 0)
                    e.wait_ge(s_f_scm, m)
                e.wait_ge(s_f_qkT, m + 1)
                for h in range(RH):
                    mm = e.matmul(sc_ps[:, h, :], qkT[:, 1, h, :], qkT[:, 0, h, :], start=True, stop=True)
                mm.then_inc(s_f_sc, 1)
                if not first:
                    e.wait_ge(s_f_mixp, m)
                e.wait_ge(s_f_pT, m + 1)
                for g in range(PG):
                    mm = e.matmul(yp_ps[:, g, :], poolT[:, g, :], pool_w[:, g, :], start=True, stop=True)
                mm.then_inc(s_f_yp, 1)
                if not first:
                    mix_half(m - 1, 1)
                    e.wait_ge(s_f_oc, m)
                e.wait_ge(s_f_qd, m + 1)
                e.wait_ge(s_f_scm, m + 1)
                slot = NT - 1 if isinstance(m, int) and m == 1 else NT if isinstance(m, int) and m == 0 else m - 1
                for h in range(RH):
                    e.matmul(o_ps[:, h, :], sc_masked[:, h, :], vg_in[:, j, h * P:(h + 1) * P], start=True, stop=False)
                    e.matmul(o_ps[:, h, :], qT_dec[:, 0, h, :], fwd_state[:, j, h, :], start=False, stop=False)
                    mm = e.matmul(o_ps[:, h, :], qT_dec[:, 1, h, :], back_states[:, slot, h, :], start=False, stop=True)
                mm.then_inc(s_f_o, 1)

            chunk_runs(e, body)
            mix_half(NT - 1, 0)
            mix_half(NT - 1, 1)


        NU = AH * LT
        S_COLS = [(c * HB, min(T, (c + 1) * HB)) for c in range((T + HB - 1) // HB)]
        PARTS = [(0, 2 * HB), (2 * HB, 3 * HB), (3 * HB, T)]
        NPART = len(PARTS)
        GROUPS = [range(4 * g, min(NT, 4 * g + 4)) for g in range((NT + 3) // 4)]
        NG = len(GROUPS)
        TORD = {0: 0, 1: 1, 2: 2, 3: 3, 4: 4, "o": 5}
        PT_SLOT = (0, 1, 2, 0, 1)
        CUT = 3 * HB
        NTO = len(TORD)

        s_q_in = [sem(f"s_q_in{j}") for j in range(2)]
        s_k_in = [sem(f"s_k_in{j}") for j in range(2)]
        s_v_in = [sem(f"s_v_in{j}") for j in range(2)]
        s_g_in = [sem(f"s_g_in{j}") for j in range(2)]
        s_held = sem("s_held")
        s_qh = sem("s_qh")
        s_qs = sem("s_qs")
        s_kh = sem("s_kh")
        s_ks = sem("s_ks")
        s_S = sem("s_S")
        s_mx = sem("s_mx")
        s_nb = sem("s_nb")
        s_exp = sem("s_exp")
        s_c = sem("s_c")
        s_comb = sem("s_comb")
        s_comb_p = sem("s_comb_p")
        s_scaled = sem("s_scaled")
        s_T = sem("s_T")
        s_Te = sem("s_Te")
        s_pv = sem("s_pv")
        s_o1 = sem("s_o1")
        s_osq = sem("s_osq")
        s_oms = sem("s_oms")
        s_ors = sem("s_ors")
        s_og = sem("s_og")
        s_ost = [sem(f"s_ost{j}") for j in range(2)]

        S_ps = ps[:, 0:5, :].rearrange("p b n -> p (b n)")
        T_ps = [ps[:, 5 + b, :].rearrange("p (k n) -> p k n", n=P) for b in range(2)]
        O_ps = ps[:, 7, 0:P]
        k_hi_s = k_hi.rearrange("p a m (s c) -> p a s m c", c=KS)
        k_lo_s = k_lo.rearrange("p a m (s c) -> p a s m c", c=KS)
        v_in_s = v_in.rearrange("p a t d -> p a (t d)").rearrange("p a (s c) -> p a s c", c=NT * P // LT)
        kT1_s = kT1.rearrange("h (m d) (s c) -> h s d m c", m=2, c=KS)
        qT1_s = qT1.rearrange("h (m d) (t n) -> h t d m n", m=2, n=P)
        v1_s = v1.rearrange("h p t d -> h p (t d)").rearrange("h p (s c) -> h s p c", c=NT * P // LT)
        g1_s = g1.rearrange("(t p) (h d) -> h t p d", p=P, d=P)
        oT1_s = oT1.rearrange("h d (t n) -> h t d n", n=P)

        def head_tile(e, u):
            if isinstance(u, int):
                return u // LT, u % LT
            h = nc.s_assert_within(u >> 4, 0, AH - 1,
                                   skip_runtime_bounds_check_because="tiles are numbered below AH * LT")
            return h, u & (LT - 1)

        def place(w, g):
            return NTO * w + (0 if isinstance(w, int) and w == NU else TORD[g])

        def bank(w, g):
            return 0 if isinstance(w, int) and w == NU else TORD[g] % 2

        def parity(h):
            return h & 1

        def has(u, lo=0, hi=NU):
            return not isinstance(u, int) or lo <= u < hi

        def ge(e, s, v):
            if not isinstance(v, int) or v > 0:
                e.wait_ge(s, v)

        def steps(e, body, cuts=()):
            for u in range(2):
                body(u, u, u)
            edges = [1, 2, *cuts, NU // 2]
            for a, b in zip(edges, edges[1:]):
                if b - a == 1:
                    for j in range(2):
                        body(2 * a + j, j, 2 * a + j)
                else:
                    with e.Fori(a, b) as i:
                        for j in range(2):
                            body(2 * i + j, j, 2 * (b - 1) + j)
            for j in range(2):
                body(NU + j, j, NU + j)

        def sp_att(e):
            def hold(s, v):
                ge(e, s, v)
                e.sem_inc(s_held, 1)

            def q(u, j, wait):
                h, t = head_tile(e, u)
                if wait:
                    hold(s_qs, u - 1)
                for d in range(2):
                    e.dma_start(q_raw[d * DH:(d + 1) * DH, j], qT1_s[h, t]).then_inc(s_q_in[j], 16)

            def k(n, j, wait):
                h, s = head_tile(e, n)
                if wait:
                    hold(s_ks, n - 1)
                for d in range(2):
                    e.dma_start(k_raw[d * DH:(d + 1) * DH, j], kT1_s[h, s]).then_inc(s_k_in[j], 16)

            def v(n, j, wait):
                h, s = head_tile(e, n)
                if wait:
                    hold(s_pv, NG * (n - LT))
                e.dma_start(v_in_s[:, parity(h), s], v1_s[h, s]).then_inc(s_v_in[j], 16)

            for n in range(2):
                q(n, n, False)
            for n in range(LT + 2):
                k(n, n % 2, n >= 2)
            for n in range(LT):
                v(n, n % 2, False)

            def body(u, j, top):
                if top + 2 < NU:
                    q(u + 2, j, True)
                if top < NU:
                    h, t = head_tile(e, u)
                    if has(u, 2):
                        hold(s_og, u - 1)
                    e.dma_start(g_in[:, j, :], g1_s[h, t]).then_inc(s_g_in[j], 16)
                if has(u, 2) and top + LT - 2 < NU:
                    v(u + (LT - 2), j, True)
                if top + LT + 2 < NU:
                    k(u + LT + 2, j, True)
                if has(u, 3, NU + 2):
                    store(u - 3, 1 - j)

            def store(w, j):
                h, t = head_tile(e, w)
                hold(s_Te, place(w + 1, "o") + 1)
                e.dma_start(oT1_s[h, t], oT_s[:, j, :]).then_inc(s_ost[j], 16)

            steps(e, body, cuts=((NU - LT - 2) // 2, (NU - LT + 2) // 2, NU // 2 - 1))
            store(NU - 1, 1)
            for s in s_ost:
                e.wait_ge(s, 8 * NU)

        def pool_att(e):
            def zeros(n):
                return zero_col[:, :].unsqueeze(2).to_broadcast([P, 2, n])

            def n_is_late(n):
                return not isinstance(n, int) or n >= 2 * LT

            def split_k(n, j):
                h, s = head_tile(e, n)
                dst = (k_hi_s[:, parity(h), s], k_lo_s[:, parity(h), s])
                if n_is_late(n):
                    e.wait_ge(s_S, 2 * NPART * (n - LT))
                e.wait_ge(s_k_in[j], 16 * (n - j) + 32)
                e.tensor_tensor(dst[0], k_raw[:, j], zeros(KS), ALU.add).then_inc(s_kh, 1)
                e.wait_ge(s_kh, n + 1)
                e.tensor_tensor(dst[1], k_raw[:, j], dst[0], ALU.subtract).then_inc(s_ks, 1)

            def split_q(u, j):
                if has(u, 2):
                    e.wait_ge(s_S, 2 * NPART * (u - 1))
                e.wait_ge(s_q_in[j], 16 * (u - j) + 32)
                e.tensor_tensor(q_st[j][:, :, :], q_raw[:, j], zeros(P), ALU.add).then_inc(s_qh, 1)
                e.wait_ge(s_qh, u + 1)
                low = slice(DH, P)
                e.tensor_tensor(q_st[j][low], q_raw[low, j], q_st[j][low], ALU.subtract).then_inc(s_qs, 1)
                e.wait_ge(s_qs, u + 1)

            for n in range(LT):
                split_k(n, n % 2)
            split_q(0, 0)

            def ratios(u, j):
                e.wait_ge(s_exp, NPART * (2 * u + 2))
                e.tensor_tensor(den_part[:, :], sums[:, j, :, 0], sums[:, j, :, 1], ALU.add).then_inc(s_c, 1)
                e.wait_ge(s_c, 5 * u + 1)
                e.tensor_tensor(denom[:, :], den_part[:, :], sums[:, j, :, 2], ALU.add).then_inc(s_c, 1)
                e.wait_ge(s_c, 5 * u + 2)
                e.tensor_tensor(rden[:, j, :], denom[:, :], minus_one[:, :], ALU.pow).then_inc(s_c, 1)
                e.tensor_tensor(lam_den[:, :], denom[:, 0:1], neg_lam[:, 0:1], ALU.mult).then_inc(s_c, 1)
                e.wait_ge(s_c, 5 * u + 4)
                e.tensor_tensor(ratio[:, j, :], lam_den[:, :], rden[:, j, 1:2], ALU.mult).then_inc(s_c, 1)

            def body(u, j, top):
                if has(u, 1, NU + 1):
                    ratios(u - 1, 1 - j)
                    e.wait_ge(s_c, 5 * u)
                    e.tensor_tensor(prob[:, 2, CUT:], prob[:, 2, CUT:], ratio[:, 1 - j, :].to_broadcast([P, T - CUT]),
                                    ALU.mult).then_inc(s_scaled, 1)
                    e.wait_ge(s_scaled, u)
                    e.tensor_tensor(prob[:, 1 - j, CUT:], prob[:, 2, CUT:], prob[:, 1 - j, CUT:], ALU.add)\
                        .then_inc(s_comb_p, 1)
                if top + 1 < NU:
                    split_q(u + 1, 1 - j)
                if has(u, 2, NU + 2):
                    e.wait_ge(s_osq, u - 1)
                    e.tensor_tensor(o_ms[:, j], o_ss[:, j], eps_col[:, 0:1], ALU.add).then_inc(s_oms, 1)
                    e.wait_ge(s_oms, u - 1)
                    e.tensor_tensor(o_rstd[:, j], o_ms[:, j], minus_half[:, 0:1], ALU.pow).then_inc(s_ors, 1)
                if top + LT < NU:
                    split_k(u + LT, j)

            steps(e, body, cuts=((NU - LT) // 2, NU // 2 - 1))

        def pe_att(e):
            def scores(u, j, m, between):
                h, _ = head_tile(e, u)
                if m == 0:
                    e.wait_ge(s_qs, u + 1)
                    e.wait_ge(s_ks, LT * (h + 1))
                for c, (a, b) in enumerate(S_COLS):
                    if c == 3:
                        between()
                    if c in (0, 2, 3):
                        ge(e, s_exp, NPART * (2 * u + m - 1) + (0, 0, 1, 2)[c] + 1 if has(u, 1) or m else 0)
                    out_ = S_ps[:, a:b]
                    e.matmul(out_, q_st[j][:, m, :], k_hi[:, parity(h), m, a:b], start=True, stop=False)
                    mm = e.matmul(out_, q_st[j][:, m, :], k_lo[:, parity(h), m, a:b], start=False, stop=True)
                    if c in (1, 2, 4):
                        mm.then_inc(s_S, 1)

            def turn(w, j, g):
                x = place(w, g)
                if g == 0:
                    e.wait_ge(s_comb, w + 1)
                if g == 3:
                    e.wait_ge(s_comb_p, w + 1)
                if g == "o":
                    if has(w, 1, NU + 1):
                        e.wait_ge(s_og, w)
                    else:
                        e.wait_ge(s_rv, 7)
                ge(e, s_Te, x - 1)
                dst = T_ps[bank(w, g)]
                if g == "o":
                    t = e.transpose(dst[:, 0, :], o_gated[:, 1 - j, :], ident[:, :])
                else:
                    for b, kt in enumerate(GROUPS[g]):
                        t = e.transpose(dst[:, b, :], prob[:, j, kt * P:(kt + 1) * P], ident[:, :])
                t.then_inc(s_T, 1)

            def times_v(w, j, g):
                h, _ = head_tile(e, w)
                if g == 0:
                    for s in s_v_in:
                        e.wait_ge(s, 8 * LT * (h + 1))
                    ge(e, s_o1, w)
                e.wait_ge(s_Te, NTO * w + TORD[g] + 1)
                for b, kt in enumerate(GROUPS[g]):
                    mm = e.matmul(O_ps, probT[:, PT_SLOT[g], b, :], v_in[:, parity(h), kt, :],
                                  start=(kt == 0), stop=(kt == NT - 1))
                mm.then_inc(s_pv, 1)

            def body(u, j, top):
                old, new = has(u, 2, NU + 2), has(u, 1, NU + 1)

                def turn_4():
                    if old:
                        turn(u - 2, j, 4)

                def turn_0():
                    if new:
                        turn(u - 1, 1 - j, 0)

                if old:
                    turn(u - 2, j, 3)
                if top < NU:
                    scores(u, j, 0, turn_4)
                else:
                    turn_4()
                if old:
                    turn(u - 2, j, "o")
                    for g in (2, 3, 4):
                        times_v(u - 2, j, g)
                if top < NU:
                    scores(u, j, 1, turn_0)
                else:
                    turn_0()
                if new:
                    turn(u - 1, 1 - j, 1)
                    turn(u - 1, 1 - j, 2)
                    times_v(u - 1, 1 - j, 0)
                    times_v(u - 1, 1 - j, 1)

            steps(e, body)
            turn(NU, 0, "o")

        def act_att(e):
            def leave(w, j, g):
                x = place(w, g)
                src = T_ps[bank(w, g)]
                if g == "o":
                    ge(e, s_ost[1 - j], 8 * (w - 2 + j))
                    e.wait_ge(s_T, x + 1)
                    e.activation(oT_s[:, 1 - j, :], src[:, 0, :], ACT.Copy).then_inc(s_Te, 1)
                    return
                ge(e, s_pv, NG * w + (-1, 0, -2, 1, 2)[g])
                e.wait_ge(s_T, x + 1)
                n = len(GROUPS[g])
                e.activation(probT[:, PT_SLOT[g], 0:n, :], src[:, 0:n, :], ACT.Copy).then_inc(s_Te, 1)

            def exps(u, j, m):
                if m == 0 and has(u, 2):
                    e.wait_ge(s_T, place(u - 2, 4) + 1)
                if m == 1:
                    ge(e, s_comb, u)
                    ge(e, s_comb_p, u)
                e.wait_ge(s_nb, 2 * u + m + 1)
                dst = prob[:, j if m == 0 else 2, :]
                for c, (a, b) in enumerate(PARTS):
                    e.activation(dst[:, a:b], S_ps[:, a:b], ACT.Exp, bias=nbias[:, j, m:m + 1],
                                 accum_out=sums[:, j, m, c:c + 1]).then_inc(s_exp, 1)

            def body(u, j, top):
                if has(u, 1, NU + 1):
                    exps(u - 1, 1 - j, 1)
                if has(u, 2, NU + 2):
                    leave(u - 2, j, 3)
                    leave(u - 2, j, 4)
                    leave(u - 2, j, "o")
                if top < NU:
                    exps(u, j, 0)
                if has(u, 2, NU + 2):
                    e.wait_ge(s_o1, u - 1)
                    e.activation(o_sq1[:, :], o_s[:, j, :], ACT.Square, scale=P ** -0.5, accum_out=o_ss[:, j])\
                        .then_inc(s_osq, 1)
                if has(u, 1, NU + 1):
                    for g in range(3):
                        leave(u - 1, 1 - j, g)

            steps(e, body)
            leave(NU, 0, "o")

        def dve_att(e):
            e.memset(o_gated[:, 1, :], 0.0).then_inc(s_rv, 1)

            def maxima(u, m, parts):
                for c in parts:
                    a, b = PARTS[c]
                    e.wait_ge(s_S, NPART * (2 * u + m) + c + 1)
                    e.tensor_reduce(amax[:, m, c:c + 1], S_ps[:, a:b], AX.X, ALU.max).then_inc(s_mx, 1)

            def bias(u, j, m):
                e.wait_ge(s_mx, NPART * (2 * u + m + 1))
                e.tensor_reduce(nbias[:, j, m:m + 1], amax[:, m, 0:NPART], AX.X, ALU.max, negate=True)\
                    .then_inc(s_nb, 1)

            def body(u, j, top):
                if top < NU:
                    maxima(u, 0, (0, 1, 2))
                    bias(u, j, 0)
                if has(u, 1, NU + 1):
                    e.wait_ge(s_c, 5 * u)
                    e.scalar_tensor_tensor(out=prob[:, 1 - j, 0:CUT], in0=prob[:, 2, 0:CUT], scalar=ratio[:, 1 - j, :],
                                           in1=prob[:, 1 - j, 0:CUT], op0=ALU.mult, op1=ALU.add).then_inc(s_comb, 1)
                if has(u, 2, NU + 2):
                    e.wait_ge(s_pv, NG * (u - 1))
                    e.tensor_scalar(o_s[:, j, :], O_ps, rden[:, j, 0:1], None, ALU.mult).then_inc(s_o1, 1)
                if top < NU:
                    maxima(u, 1, (0, 1, 2))
                    bias(u, j, 1)
                if has(u, 2, NU + 2):
                    e.wait_ge(s_g_in[j], 8 * (u - j))
                    ge(e, s_T, place(u - 3, "o") + 1)
                    e.wait_ge(s_ors, u - 1)
                    e.scalar_tensor_tensor(out=o_gated[:, j, :], in0=o_s[:, j, :], scalar=o_rstd[:, j],
                                           in1=g_in[:, j, :], op0=ALU.mult, op1=ALU.mult).then_inc(s_og, 1)

            steps(e, body)


        def sp_stored(e, p):
            for s in s_st:
                e.wait_ge(s, 8 * base(p, lambda r: not keeps_T(r)))
            if base(p, keeps_T):
                e.wait_ge(s_yst, 16 * base(p, keeps_T))

        @block.sync
        def _(e):
            sp_setup(e)
            stage_end(e, 1)
            for p in range(3):
                sp_pass(e, p)
            sp_stored(e, 3)
            stage_end(e, 2)
            sp_ret(e)
            stage_end(e, 3)
            for p in range(3, 8):
                sp_pass(e, p)
            sp_stored(e, 8)
            stage_end(e, 4)
            sp_att(e)
            stage_end(e, 5)
            sp_pass(e, 8)
            sp_stored(e, 9)

        @block.scalar
        def _(e):
            act_setup(e)
            stage_end(e, 1)
            for p in range(3):
                act_pass(e, p)
            stage_end(e, 2)
            act_ret(e)
            stage_end(e, 3)
            for p in range(3, 8):
                act_pass(e, p)
            stage_end(e, 4)
            act_att(e)
            stage_end(e, 5)
            act_pass(e, 8)

        @block.tensor
        def _(e):
            pe_setup(e)
            stage_end(e, 1)
            for p in range(3):
                pe_pass(e, p)
            stage_end(e, 2)
            pe_ret(e)
            stage_end(e, 3)
            for p in range(3, 8):
                pe_pass(e, p)
            stage_end(e, 4)
            pe_att(e)
            stage_end(e, 5)
            pe_pass(e, 8)

        @block.vector
        def _(e):
            dve_setup(e)
            stage_end(e, 1)
            for p in range(3):
                dve_pass(e, p)
            stage_end(e, 2)
            dve_ret(e)
            stage_end(e, 3)
            for p in range(3, 8):
                dve_pass(e, p)
            stage_end(e, 4)
            dve_att(e)
            stage_end(e, 5)
            dve_pass(e, 8)

        @block.gpsimd
        def _(e):
            pool_setup(e)
            stage_end(e, 1)
            for p in range(3):
                pool_pass(e, p)
            stage_end(e, 2)
            pool_ret(e)
            stage_end(e, 3)
            for p in range(3, 8):
                pool_pass(e, p)
            stage_end(e, 4)
            pool_att(e)
            stage_end(e, 5)
            pool_pass(e, 8)

_WEIGHTS = ["ada_w", "ada_b", "norm_post", "ev_w_in", "ev_w_out", "ret_decay_logit", "pool_w", "pool_scale",
            "od_w_in", "od_w_out", "diff_lambda", "diff_subln"]


def laid_out(inputs):
    a = {n: np.ascontiguousarray(inputs[n]) for n in _WEIGHTS}
    a["x_all"] = np.concatenate([np.asarray(inputs["ctx"])[0], np.asarray(inputs["x"])[0]])
    cond = np.stack([np.asarray(inputs["c_ctx"]), np.asarray(inputs["c"])[0]])
    a["cond"] = np.ascontiguousarray(cond.reshape(2, KC, P).transpose(2, 1, 0))
    a["npre"] = np.ascontiguousarray(np.asarray(inputs["norm_pre"]).reshape(2, KC, P).transpose(2, 0, 1))
    a["adab_cols"] = np.ascontiguousarray(np.asarray(inputs["ada_b"]).reshape(2, 3 * KC, P).transpose(2, 0, 1))
    a.update(host_constants())
    return a


def kernel(**inputs):
    from concourse import bacc
    from concourse.bass_utils import run_bass_kernel_spmd

    nc = bacc.Bacc("TRN2", target_bir_lowering=False, num_devices=1, dynamic_dma_scratch_size=1024)
    arrays = {f"in_{n}": a for n, a in laid_out(inputs).items()}
    aps = {n[3:]: nc.dram_tensor(n, a.shape, mybir.dt.from_np(a.dtype), kind="ExternalInput").ap()
           for n, a in arrays.items()}
    out = nc.dram_tensor("out_0", (1, SEQ, D), F32, kind="ExternalOutput").ap()
    build(nc, aps, out)
    r = run_bass_kernel_spmd(nc, [arrays], core_ids=[0])
    return r.results[0]["out_0"]
```

```python
import math
from contextlib import ExitStack

import numpy as np

import concourse.bass as bass
from concourse import mybir

F32 = mybir.dt.float32
F32R = mybir.dt.float32r
ALU = mybir.AluOpType
ACT = mybir.ActivationFunctionType
AX = mybir.AxisListType.X

P = 128
D = 1024
KC = D // P
SEQ, CTX = 2048, 256
T = SEQ + CTX
NT, CT, LT = T // P, CTX // P, SEQ // P
EPS = 1e-6
GRID_W = 64
ROPE_BASE = 10000.0
RH = 4
PG = 4
POOL_WINDOWS = (2, 4, 8, 16)
HALO = 16
DH = 64
AH = 8
LAM_INIT = 0.8 - 0.6 * math.exp(-0.3 * 1)
KSCALE = float(P) ** -0.5
ASCALE = float(DH) ** -0.5
MID_PAD = 1700
ADA_SLOTS = 4
HB = 512

PASSES = [
    dict(name="qk0", tiles=(0, NT), src="norm", layer=0, post="rope", rope=0),
    dict(name="vg0", tiles=(0, NT), src="load", layer=0, post="gate"),
    dict(name="pg0", tiles=(0, NT), src="load", layer=0, post="gate"),
    dict(name="out0", tiles=(0, NT), src="load", layer=0, post="residual"),
    dict(name="k1", tiles=(0, NT), src="norm", layer=1, post="rope", rope=1),
    dict(name="v1", tiles=(0, NT), src="load", layer=1, post="copy"),
    dict(name="q1", tiles=(CT, LT), src="load", layer=1, post="rope", rope=1),
    dict(name="g1", tiles=(CT, LT), src="load", layer=1, post="silu"),
    dict(name="out1", tiles=(CT, LT), src="load", layer=1, post="residual"),
]
NP_ = len(PASSES)


def tiles_before(p, want=lambda q: True):
    return sum(q["tiles"][1] for q in PASSES[:p] if want(q))


def host_constants():
    rows = np.repeat(np.arange(SEQ // GRID_W), GRID_W).astype(np.float32)
    cols = np.tile(np.arange(GRID_W), SEQ // GRID_W).astype(np.float32)

    def rope(head):
        quarter = head // 4
        da = head // 2
        freqs = np.float32(ROPE_BASE) ** (-np.arange(quarter, dtype=np.float32) * np.float32(2.0) / np.float32(da))
        c = np.ones((T, 2, 2, quarter), np.float32)
        s = np.zeros((T, 2, 2, quarter), np.float32)
        for a, pos in enumerate((rows, cols)):
            ang = pos[:, None] * freqs[None, :]
            c[CTX:, a, :, :] = np.cos(ang)[:, None, :]
            s[CTX:, a, 0, :] = -np.sin(ang)
            s[CTX:, a, 1, :] = np.sin(ang)
        return np.stack([c.reshape(T, head), s.reshape(T, head)], 1).reshape(NT, P, 2 * head)

    j, i = np.meshgrid(np.arange(P, dtype=np.float32), np.arange(P, dtype=np.float32), indexing="ij")
    rel = np.stack([np.maximum(i - j, 0), np.maximum(j - i, 0),
                    KSCALE * (i >= j), KSCALE * (j > i)], 1).astype(np.float32)
    t = np.arange(P, dtype=np.float32)
    dec_rows = np.broadcast_to(np.stack([t + 1, P - t]), (P, 2, P)).astype(np.float32)
    dec_cols = np.stack([P - 1 - t, t], 1).astype(np.float32)
    own = np.zeros((P, 3, PG, P), np.float32)
    halo = np.zeros((2 * HALO, 3, PG, P), np.float32)
    for v in range(3):
        for g, win in enumerate(POOL_WINDOWS):
            for t in range(P):
                lo, hi = t - win // 2, t + win // 2 - 1
                if v == 1:
                    lo = max(lo, 0)
                if v == 2:
                    hi = min(hi, P - 1)
                w = np.float32(1.0) / np.float32(hi - lo + 1)
                for s in range(lo, hi + 1):
                    if s < 0:
                        halo[HALO + s, v, g, t] = w
                    elif s >= P:
                        halo[HALO + s - P, v, g, t] = w
                    else:
                        own[s, v, g, t] = w
                own[t, v, g, t] -= 1.0
    return {
        "ident": np.eye(P, dtype=np.float32), "rope0": rope(P), "rope1": rope(DH), "rel": rel.astype(np.float32),
        "dec_rows": np.ascontiguousarray(dec_rows), "dec_cols": dec_cols, "pool_own": own, "pool_halo": halo,
    }


def row_broadcast(row):
    return row.partition_broadcast(P)


def build(nc, A, out):
    def dram(name, shape):
        return nc.dram_tensor(name, shape, F32, kind="Internal").ap()

    hT = [dram("hT0", (NT, P, KC, P)), dram("hT1", (NT, P, KC, P))]
    qk0 = dram("qk0", (NT, P, D))
    vg0 = dram("vg0", (NT, P, D))
    pg0 = dram("pg0", (T, D))
    mixT = dram("mixT", (NT, P, KC, P))
    back_st = dram("back_st", (NT, P, RH, P))
    x1 = dram("x1", (T, D))
    kT1 = dram("kT1", (AH, P, T))
    qT1 = dram("qT1", (AH, P, SEQ))
    v1 = dram("v1", (AH, P, NT, P))
    g1 = dram("g1", (SEQ, D))
    oT1 = dram("oT1", (AH, P, SEQ))

    w_in = [A["ev_w_in"], A["ev_w_in"], A["ev_w_in"], A["ev_w_out"],
            A["od_w_in"], A["od_w_in"], A["od_w_in"], A["od_w_in"], A["od_w_out"]]
    w_col = [0, 1, 2, 0, 1, 2, 0, 3, 0]

    def weight_chunk(p, k):
        return w_in[p][0].rearrange("(k c) (m n) -> k c m n", c=P, n=D)[k, :, w_col[p], :]

    ctx = ExitStack()

    def sb(name, shape, dt=F32, at=ctx):
        return at.enter_context(nc.sbuf_tensor(name, shape, dt))

    def sem(name):
        return ctx.enter_context(nc.semaphore(name))

    with ctx:
        ident = sb("ident_s", [P, P])
        cond = sb("cond_s", [P, KC, 2])
        cond_silu = sb("cond_silu", [P, KC, 2])
        npre = sb("npre_s", [P, 2, KC])
        adab = sb("adab_s", [P, 2, 3 * KC])
        shift = sb("shift", [P, 2, KC, 2])
        scale = sb("scale", [P, 2, KC, 2])
        gate_post = sb("gate_post", [P, 3, D])
        lam_in = sb("lam_in", [P, 4, DH])
        lam_prod = sb("lam_prod", [P, DH])
        lam_sum = sb("lam_sum", [P, 2])
        lam_exp = sb("lam_exp", [P, 2])
        neg_lam = sb("neg_lam", [P, 2])
        subln = sb("subln_s", [P, 2, P])
        minus_half = sb("minus_half", [P, RH])
        eps_col = sb("eps_col", [P, RH])
        zero_col = sb("zero_col", [P, 1])
        minus_one = sb("minus_one", [P, 2])
        dec_cols = sb("dec_cols_s", [P, 2])
        log_g = sb("log_g", [P, 2, RH])
        log_e = sb("log_e", [P, 2, RH])
        k_arg = sb("k_arg", [P, 2, RH])
        k_dec = sb("k_dec", [P, 2, RH])
        c_dec = sb("c_dec", [P, 2, RH])
        ss = sb("ss", [P, 2, 1])
        ms = sb("ms", [P, 2, 1])
        rstd = sb("rstd", [P, 2, 1])
        ss2 = sb("ss2", [P, 2, 1])
        ms2 = sb("ms2", [P, 2, 1])
        rstd2 = sb("rstd2", [P, 2, 1])

        set1 = ExitStack()
        ctx.enter_context(set1)
        setup_bufs = ExitStack()
        ada = sb("ada", [P, ADA_SLOTS, 3 * D], at=setup_bufs)
        ones = sb("ones", [P, P], at=setup_bufs)
        adab_row = sb("adab_row", [P, D], at=setup_bufs)
        npost_row = sb("npost_row", [P, D], at=setup_bufs)
        setup_bufs.close()
        whi = [None, None]
        wlo = [None, None]
        whi[1] = sb("whi1", [P, KC, D], F32R, set1)
        wlo[1] = sb("wlo1", [P, KC, D], F32R, set1)
        mid = ExitStack()
        w_raw = sb("w_raw", [P, D], at=mid)
        a_raw = sb("a_raw", [P, 2, KC, P], at=mid)
        a_hi = [sb(f"a_hi{j}", [P, KC, P], F32R, mid) for j in range(2)]
        a_lo = [sb(f"a_lo{j}", [P, KC, P], F32R, mid) for j in range(2)]
        x_in = sb("x_in_s", [P, 2, D], at=mid)
        x_n = sb("x_n", [P, D], at=mid)
        x_sq = sb("x_sq", [P, D], at=mid)
        rope_in = sb("rope_in", [P, 2, 2 * P], at=mid)
        t_cos = sb("t_cos", [P, D], at=mid)
        t_sin = sb("t_sin", [P, D], at=mid)
        y_out = sb("y_out", [P, 2, D], at=mid)
        yT = sb("yT", [P, KC, P], at=mid)
        sb("pad", [P, MID_PAD], at=mid)
        set0 = ExitStack()
        whi[0] = sb("whi0", [P, KC, D], F32R, set0)
        wlo[0] = sb("wlo0", [P, KC, D], F32R, set0)
        set0.close()
        mid_end = nc.sbuf_bytes_remaining
        mid.close()

        ret = ExitStack()
        rel = sb("rel_s", [P, 4, P], at=ret)
        dec_rows = sb("dec_rows_s", [P, 2, P], at=ret)
        e_rel = sb("e_rel", [P, 2, RH, P], at=ret)
        decay_mask = sb("decay_mask", [P, RH, P], at=ret)
        mask_b = sb("mask_b", [P, RH, P], at=ret)
        q_dec = sb("q_dec", [P, 2, RH, P], at=ret)
        pool_own = sb("pool_own_s", [P, 3, PG, P], at=ret)
        pool_halo = sb("pool_halo_s", [2 * HALO, 3, PG, P], at=ret)
        pool_w = sb("pool_w_s", [P, PG, P], at=ret)
        pool_scale = sb("pool_scale_s", [P, PG * P], at=ret)
        back_in = sb("back_in", [P, 2, RH, P], at=ret)
        fwd_state = sb("fwd_state", [P, 2, RH, P], at=ret)
        qk_in = sb("qk_in", [P, 2, D], at=ret)
        vg_in = sb("vg_in", [P, 2, D], at=ret)
        pg_in = sb("pg_in", [P, 2, D], at=ret)
        halo_in = sb("halo_in", [2 * HALO, 2, PG * P], at=ret)
        k_scaled = sb("k_scaled", [P, 2, RH, P], at=ret)
        qkT = sb("qkT", [P, 2, RH, P], at=ret)
        qT_dec = sb("qT_dec", [P, 2, 2, RH, P], at=ret)
        sc_masked = sb("sc_masked", [P, 2, RH, P], at=ret)
        head_sum = sb("head_sum", [P, RH], at=ret)
        head_mean = sb("head_mean", [P, RH], at=ret)
        o_cent = sb("o_cent", [P, RH, P], at=ret)
        o_sq = sb("o_sq", [P, RH, P], at=ret)
        head_var = sb("head_var", [P, RH], at=ret)
        head_var2 = sb("head_var2", [P, RH], at=ret)
        head_rstd = sb("head_rstd", [P, RH], at=ret)
        o_norm = sb("o_norm", [P, RH, P], at=ret)
        mix = sb("mix", [P, KC, P], at=ret)
        gate_scaled = sb("gate_scaled", [P, PG * P], at=ret)
        poolT = sb("poolT", [P, PG, P], at=ret)
        mixT_s = sb("mixT_s", [P, KC, P], at=ret)
        ret.close()
        set1.close()

        att = ExitStack()
        k_hi = sb("k_hi", [P, 2, 2, T], F32R, att)
        k_lo = sb("k_lo", [P, 2, 2, T], F32R, att)
        KS = T // LT
        k_raw = sb("k_raw", [P, 2, 2, KS], at=att)
        v_in = sb("v_in", [P, 2, NT, P], at=att)
        q_raw = sb("q_raw", [P, 2, 2, P], at=att)
        q_st = [sb(f"q_st{j}", [P, 2, P], F32R, att) for j in range(2)]
        prob = sb("prob", [P, 3, T], at=att)
        probT = sb("probT", [P, 3, 4, P], at=att)
        g_in = sb("g_in", [P, 2, P], at=att)
        amax = sb("amax", [P, 2, 3], at=att)
        nbias = sb("nbias", [P, 2, 2], at=att)
        sums = sb("sums", [P, 2, 2, 3], at=att)
        den_part = sb("den_part", [P, 2], at=att)
        denom = sb("denom", [P, 2], at=att)
        lam_den = sb("lam_den", [P, 1], at=att)
        rden = sb("rden", [P, 2, 2], at=att)
        ratio = sb("ratio", [P, 2, 1], at=att)
        o_s = sb("o_s", [P, 2, P], at=att)
        o_sq1 = sb("o_sq1", [P, P], at=att)
        o_ss = sb("o_ss", [P, 2, 1], at=att)
        o_ms = sb("o_ms", [P, 2, 1], at=att)
        o_rstd = sb("o_rstd", [P, 2, 1], at=att)
        o_gated = sb("o_gated", [P, 2, P], at=att)
        oT_s = sb("oT_s", [P, 2, P], at=att)
        assert nc.sbuf_bytes_remaining >= mid_end, "attention runs into weight set 0"
        att.close()

        ps = ctx.enter_context(nc.psum_tensor("ps", [P, 8, HB], F32))
        y_ps = [ps[:, 2 * j:2 * j + 2, :] for j in range(2)]
        tp_ps = [ps[:, 4 + 2 * j:6 + 2 * j, :] for j in range(2)]

        s_const = sem("s_const")
        s_ada = [sem(f"s_ada{j}") for j in range(ADA_SLOTS)]
        s_ada_used = sem("s_ada_used")
        s_ada_acc = sem("s_ada_acc")
        s_mod_rows = sem("s_mod_rows")
        s_mod_cols = sem("s_mod_cols")
        s_gates = sem("s_gates")
        s_set = sem("s_set")
        s_sete = sem("s_sete")
        s_rows = sem("s_rows")
        s_stage = sem("s_stage")
        s_w_in = sem("s_w_in")
        s_w_hi = sem("s_w_hi")
        s_w_split = sem("s_w_split")
        s_a_in = [sem(f"s_a_in{j}") for j in range(2)]
        s_x_in = [sem(f"s_x_in{j}") for j in range(2)]
        s_rope_in = [sem(f"s_rope_in{j}") for j in range(2)]
        s_ss = sem("s_ss")
        s_ms = sem("s_ms")
        s_rstd = sem("s_rstd")
        s_xn = sem("s_xn")
        s_xT = sem("s_xT")
        s_mo = sem("s_mo")
        s_hi = sem("s_hi")
        s_split = sem("s_split")
        s_mm = sem("s_mm")
        s_tsin = sem("s_tsin")
        s_y = sem("s_y")
        s_y2 = sem("s_y2")
        s_yTp = sem("s_yTp")
        s_yTs = sem("s_yTs")
        s_st = [sem(f"s_st{j}") for j in range(2)]
        s_hst = [sem(f"s_hst{j}") for j in range(2)]
        s_yst = sem("s_yst")
        s_ss2 = sem("s_ss2")
        s_ms2 = sem("s_ms2")
        s_rstd2 = sem("s_rstd2")
        s_res = sem("s_res")

        block = ctx.enter_context(nc.Block())

        def is_norm(q):
            return q["src"] == "norm"

        def is_load(q):
            return q["src"] == "load"

        def is_rope(q):
            return q["post"] == "rope"

        def has_x(q):
            return is_norm(q) or q["post"] == "residual"

        def is_resid(q):
            return q["post"] == "residual"

        def keeps_T(q):
            return is_rope(q) and q["rope"] == 1

        def in_y_out(q):
            return not keeps_T(q)

        def pairs(e, p, body):
            n = PASSES[p]["tiles"][1] // 2
            body(0, True, False)
            with e.Fori(1, n - 1) as i:
                body(i, False, False)
            body(n - 1, False, True)

        def base(p, want=lambda q: True):
            return tiles_before(p, want)

        def stage_end(e, k):
            e.drain().then_inc(s_stage, 1)
            e.wait_ge(s_stage, 5 * k)


        N_CONST = 8
        w_first = [w_raw[:, :], x_n[:, :], x_sq[:, :], t_cos[:, :], t_sin[:, :], y_out[:, 0, :], y_out[:, 1, :],
                   yT.rearrange("p k n -> p (k n)")]
        mod_rows = a_raw.rearrange("p j k n -> p (j k n)")[0:2, :]
        mod_cols = ps[:, 0, 0:4 * KC].rearrange("p (b s) -> p b s", s=2)

        def sp_setup(e):
            e.dma_start(cond[:, :, :], A["cond"]).then_inc(s_const, 16)
            e.dma_start(ident[:, :], A["ident"]).then_inc(s_const, 16)
            e.dma_start(npre[:, :, :], A["npre"]).then_inc(s_const, 16)
            e.dma_start(adab[:, :, :], A["adab_cols"]).then_inc(s_const, 16)
            e.dma_start(lam_in[:, :, :], row_broadcast(A["diff_lambda"][0])).then_inc(s_const, 16)
            e.dma_start(log_e[:, :, :], row_broadcast(A["ret_decay_logit"][0])).then_inc(s_const, 16)
            e.dma_start(dec_cols[:, :], A["dec_cols"]).then_inc(s_const, 16)
            e.dma_start(subln[:, 0, :], row_broadcast(A["diff_subln"][0])).then_inc(s_const, 16)

            def rows(l):
                e.dma_start(adab_row[:, :], row_broadcast(A["ada_b"][l, 2 * D:])).then_inc(s_rows, 16)
                e.dma_start(npost_row[:, :], row_broadcast(A["norm_post"][l])).then_inc(s_rows, 16)

            rows(0)
            for n in range(2 * KC):
                l, k = n // KC, n % KC
                if n == KC:
                    for c in range(KC):
                        e.dma_start(w_first[c], weight_chunk(0, c)).then_inc(s_w_in, 16)
                if n >= ADA_SLOTS:
                    e.wait_ge(s_ada_used, n - ADA_SLOTS + 1)
                    e.wait_ge(s_ada_acc, n - ADA_SLOTS + 1)
                e.dma_start(ada[:, n % ADA_SLOTS, :], A["ada_w"][l, k * P:(k + 1) * P, :])\
                    .then_inc(s_ada[n % ADA_SLOTS], 16)
            e.wait_ge(s_set, 17)
            rows(1)
            for j in range(2):
                sp_load(e, 0, j, 0, j, True)

        def act_setup(e):
            def act_rows(l):
                e.wait_ge(s_ada_used, KC * (l + 1))
                e.activation(mod_rows, ps[0:2, 0:4, :].rearrange("p b n -> p (b n)"), ACT.Copy).then_inc(s_mod_rows, 1)

            e.wait_ge(s_const, 16 * N_CONST)
            e.activation(cond_silu[:, :, :], cond[:, :, :], ACT.Silu).then_inc(s_sete, 1)
            e.wait_ge(s_set, 7)
            e.activation(lam_exp[:, :], lam_sum[:, :], ACT.Exp).then_inc(s_sete, 1)
            e.activation(log_g[:, :, :], log_e[:, :, :], ACT.Exp).then_inc(s_sete, 1)
            e.wait_ge(s_set, 12)
            e.activation(c_dec[:, :, :], log_g[:, :, :], ACT.Exp, scale=float(P))
            e.activation(k_dec[:, :, :], k_arg[:, :, :], ACT.Exp).then_inc(s_sete, 1)
            act_rows(0)
            e.wait_ge(s_w_in, 16 * KC)
            for c in range(KC):
                e.activation(whi[0][:, c, :], w_first[c], ACT.Copy).then_inc(s_w_hi, 1)
            act_rows(1)

        def pe_setup(e):
            e.wait_ge(s_sete, 1)
            e.wait_ge(s_set, 3)
            for l in range(2):
                for k in range(KC):
                    n = KC * l + k
                    e.wait_ge(s_ada[n % ADA_SLOTS], 16 * (n // ADA_SLOTS + 1))
                    w = ada[:, n % ADA_SLOTS, :]
                    if l and k == 0:
                        e.wait_ge(s_set, 19)
                    for b in range(4):
                        mm = e.matmul(ps[0:2, b, :], cond_silu[:, k, :], w[:, b * HB:(b + 1) * HB],
                                      start=(k == 0), stop=(k == KC - 1))
                    mm.then_inc(s_ada_used, 1)
                e.wait_ge(s_mod_rows, l + 1)
                for b in range(2 * KC):
                    t = e.transpose(mod_cols[:, b, :], mod_rows[:, b * P:(b + 1) * P], ident[0:2, 0:2])
                t.then_inc(s_mod_cols, 1)
                e.wait_ge(s_ada_acc, KC * (l + 1))
                for m in range(2 - l):
                    for b in range(2):
                        mm = e.matmul(ps[:, 4 + 2 * m + b, :], ones[:, :],
                                      gate_post[:, 2 * l + m, b * HB:(b + 1) * HB], start=True, stop=True)
                mm.then_inc(s_gates, 1)

        def dve_setup(e):
            n = 0

            def step(ins):
                nonlocal n
                n += 1
                ins.then_inc(s_set, 1)
                e.wait_ge(s_set, n)

            e.sem_inc(s_split, 2)
            e.sem_inc(s_mm, 2)
            step(e.memset(minus_half[:, :], -0.5))
            step(e.memset(eps_col[:, :], EPS))
            e.wait_ge(s_sete, 1)
            step(e.memset(ones[:, :], 1.0))
            e.wait_ge(s_const, 16 * N_CONST)
            for m in range(2):
                step(e.tensor_tensor(lam_prod[:, :], lam_in[:, 2 * m, :], lam_in[:, 2 * m + 1, :], ALU.mult))
                step(e.tensor_reduce(lam_sum[:, m:m + 1], lam_prod[:, :], AX.X, ALU.add))
            e.wait_ge(s_sete, 2)
            step(e.tensor_tensor(neg_lam[:, 1:2], lam_exp[:, 1:2], lam_exp[:, 0:1], ALU.subtract))
            step(e.tensor_scalar(neg_lam[:, 0:1], neg_lam[:, 1:2], 1.0, -LAM_INIT, ALU.mult, ALU.add))
            step(e.tensor_scalar(subln[:, 1, :], subln[:, 0, :], 1.0 - LAM_INIT, None, ALU.mult))
            e.wait_ge(s_sete, 3)
            step(e.tensor_scalar(log_g[:, :, :], log_g[:, :, :], -1.0, None, ALU.mult))
            for d in range(2):
                ins = e.tensor_scalar(k_arg[:, d, :], log_g[:, d, :], dec_cols[:, d:d + 1], None, ALU.mult)
            step(ins)
            e.wait_ge(s_sete, 4)
            step(e.tensor_scalar(k_dec[:, :, :], k_dec[:, :, :], KSCALE, None, ALU.mult))
            for l in range(2):
                for k in range(KC):
                    c = KC * l + k
                    e.wait_ge(s_ada[c % ADA_SLOTS], 16 * (c // ADA_SLOTS + 1))
                    w = ada[:, c % ADA_SLOTS, 2 * D:]
                    if k:
                        e.wait_ge(s_ada_acc, c)
                    for m in range(2 - l):
                        dst, factor = gate_post[:, 2 * l + m, :], cond_silu[:, k, l + m:l + m + 1]
                        if k == 0:
                            ins = e.tensor_scalar(dst, w, factor, None, ALU.mult)
                        else:
                            ins = e.scalar_tensor_tensor(out=dst, in0=w, scalar=factor, in1=dst,
                                                         op0=ALU.mult, op1=ALU.add)
                    ins.then_inc(s_ada_acc, 1)
                    if l:
                        if k == 0:
                            e.wait_ge(s_w_in, 16 * KC)
                        e.wait_ge(s_w_hi, k + 1)
                        e.tensor_tensor(wlo[0][:, k, :], w_first[k], whi[0][:, k, :], ALU.subtract)\
                            .then_inc(s_w_split, 1)
                e.wait_ge(s_rows, 32 * (l + 1))
                e.wait_ge(s_gates, l + 1)
                for m in range(2 - l):
                    gate = ps[:, 4 + 2 * m:6 + 2 * m, :].rearrange("p b n -> p (b n)")
                    dst = gate_post[:, 2 * l + m, :]
                    step(e.tensor_tensor(dst, gate, adab_row[:, :], ALU.add))
                    step(e.tensor_tensor(dst, dst, npost_row[:, :], ALU.mult))
                e.wait_ge(s_mod_cols, l + 1)
                cols = ps[:, 0, 0:4 * KC].rearrange("p (h k s) -> p h k s", h=2, k=KC)
                for h, dst in enumerate((shift, scale)):
                    bias = adab[:, l, h * KC:(h + 1) * KC].unsqueeze(2).to_broadcast([P, KC, 2])
                    step(e.tensor_tensor(dst[:, l], cols[:, h], bias, ALU.add))
                step(e.scalar_tensor_tensor(out=scale[:, l], in0=scale[:, l], scalar=1.0,
                                            in1=npre[:, l].unsqueeze(2).to_broadcast([P, KC, 2]),
                                            op0=ALU.add, op1=ALU.mult))
            step(e.memset(zero_col[:, :], 0.0))
            step(e.memset(minus_one[:, :], -1.0))

        def pool_setup(e):
            pass


        BACK = 2
        s_b_in = [sem(f"s_b_in{j}") for j in range(2)]
        s_b_k = sem("s_b_k")
        s_b_U = sem("s_b_U")
        s_b_S = sem("s_b_S")
        s_b_st = [sem(f"s_b_st{j}") for j in range(2)]
        s_b_held = sem("s_b_held")

        def heads(x):
            return x.unsqueeze(2).to_broadcast([P, RH, P])

        def by_head(x):
            return x.rearrange("p (h n) -> p h n", n=P)

        def back_state(j):
            return by_head(x_sq[:, j * HB:(j + 1) * HB])

        def back_scaled(j):
            return by_head(x_n[:, j * HB:(j + 1) * HB])

        def back_U(j):
            return by_head(ps[:, 4 + j, :])

        def has(u, lo, hi):
            return not isinstance(u, int) or lo <= u < hi

        def ge(e, s, v):
            if not isinstance(v, int) or v > 0:
                e.wait_ge(s, v)

        def back_step(i, j):
            if isinstance(i, int):
                return 1 - j if i == 0 else NT + 1 - 2 * i - j
            return (-2) * i + (NT + 1 - j)

        def sp_back_load(e, i, j):
            if isinstance(i, int) and i == 0 and j == 0:
                for s in s_st:
                    e.wait_ge(s, 8 * base(BACK, lambda r: not keeps_T(r)))
                e.wait_ge(s_xn, base(BACK, is_norm))
            c = back_step(i, j)
            if not isinstance(i, int) or i:
                e.wait_ge(s_b_U, 2 * i + (j - 1))
                e.sem_inc(s_b_held, 1)
            e.dma_start(x_in[:, j, 0:HB], qk0[c, :, HB:]).then_inc(s_b_in[j], 16)
            e.dma_start(x_in[:, j, HB:], vg0[c, :, 0:HB]).then_inc(s_b_in[j], 16)

        def sp_back_store(e, m, j):
            e.wait_ge(s_b_S, m + 1)
            e.sem_inc(s_b_held, 1)
            e.dma_start(back_st[m], back_state(j)).then_inc(s_b_st[j], 16)

        def pool_back(e, i, j):
            if not isinstance(i, int) or i:
                e.wait_ge(s_b_U, 2 * i + (j - 1))
            e.wait_ge(s_b_in[j], 32 * (i + 1))
            e.tensor_tensor(back_scaled(j), by_head(x_in[:, j, 0:HB]), heads(k_dec[:, 1, :]), ALU.mult)\
                .then_inc(s_b_k, 1)

        def pe_back(e, m, j):
            ge(e, s_b_S, m)
            e.wait_ge(s_b_k, m + 1)
            for h in range(RH):
                mm = e.matmul(back_U(j)[:, h, :], back_scaled(j)[:, h, :], x_in[:, j, HB + h * P:HB + (h + 1) * P],
                              start=True, stop=True)
            mm.then_inc(s_b_U, 1)

        def dve_back(e, m, j):
            if has(m, 1, NT):
                e.wait_ge(s_b_st[1 - j], 8 * (m + j))
            e.wait_ge(s_b_S, m + 1)
            e.wait_ge(s_b_U, m + 1)
            for h in range(RH):
                ins = e.scalar_tensor_tensor(out=back_state(1 - j)[:, h, :], in0=back_state(j)[:, h, :],
                                             scalar=c_dec[:, 1, h:h + 1], in1=back_U(j)[:, h, :],
                                             op0=ALU.mult, op1=ALU.add)
            ins.then_inc(s_b_S, 1)


        def wait_y_out_free(e, p, L, i, j, first):
            prev = PASSES[p] if not first else PASSES[p - 1] if p else None
            if prev is None:
                return
            if keeps_T(prev):
                e.wait_ge(s_yTp, base(p, keeps_T) + (0 if first else L - 1))
            else:
                e.wait_ge(s_st[j], 16 * (base(p, lambda q: not keeps_T(q)) // 2 + (0 if first else i)))

        def act_reads(q):
            return q["post"] in ("gate", "silu")

        def wait_y_ps_free(e, p, L, first):
            prev = PASSES[p] if not first else PASSES[p - 1] if p else None
            if prev is None:
                return
            back = 0 if first else L - 1
            if is_rope(prev):
                e.wait_ge(s_tsin, base(p, is_rope) + back)
            if prev["post"] in ("gate", "copy"):
                e.wait_ge(s_y, base(p) + back)
            if prev["post"] == "silu":
                e.wait_ge(s_y2, base(p, act_reads) + back)
            if is_resid(prev):
                e.wait_ge(s_res, base(p, is_resid) + back)

        def early(p):
            return p < NP_ and is_load(PASSES[p]) and not is_resid(PASSES[p])

        def ahead(p):
            return 0 < p < NP_ and is_norm(PASSES[p])


        def sp_weights(e, p, i):
            if not (isinstance(i, int) and 8 * p + i == 0):
                e.wait_ge(s_w_split, 8 * p + i)
            e.dma_start(w_raw[:, :], weight_chunk(p, i)).then_inc(s_w_in, 16)

        def sp_load(e, p, L, i, j, first):
            q = PASSES[p]
            t0 = q["tiles"][0]
            if is_norm(q):
                if not first:
                    e.wait_ge(s_xn, base(p, is_norm) + L - 1)
                elif base(p, has_x):
                    e.wait_ge(s_y, base(p) + j - 1)
                if q["layer"]:
                    e.wait_ge(s_st[j], 16 * (base(p - 1, lambda r: not keeps_T(r)) // 2 + 1) if first
                              else 8 * base(p, lambda r: not keeps_T(r)))
                src = A["x_all"] if q["layer"] == 0 else x1
                e.dma_start(x_in[:, j, :], src.rearrange("(t p) d -> t p d", p=P)[L + t0]).then_inc(s_x_in[j], 16)
                return
            e.wait_ge(s_split, base(p) + L + 1)
            if first and j == 0 and is_norm(PASSES[p - 1]):
                for s in s_hst:
                    e.wait_ge(s, 8 * base(p, is_norm))
            if p == NP_ - 1:
                src = oT1.rearrange("h d (t p) -> t d h p", p=P)[L]
            elif is_resid(q):
                src = mixT[L]
            else:
                src = hT[q["layer"]][L + t0]
            e.dma_start(a_raw[:, j], src).then_inc(s_a_in[j], 16)

        def sp_late(e, p, L, i, j, first):
            q = PASSES[p]
            t0 = q["tiles"][0]
            if is_rope(q):
                w = rope_w(q)
                if not first or base(p, is_rope):
                    e.wait_ge(s_tsin, base(p, is_rope) + (L - 1 if not first else 0))
                e.dma_start(rope_in[:, j, 0:w], A[f"rope{q['rope']}"][L + t0]).then_inc(s_rope_in[j], 16)
            if is_resid(q):
                if not first:
                    e.wait_ge(s_y, base(p) + L - 1)
                else:
                    e.wait_ge(s_xn, base(p, is_norm))
                src = A["x_all"] if q["layer"] == 0 else x1
                e.dma_start(x_in[:, j, :], src.rearrange("(t p) d -> t p d", p=P)[L + t0]).then_inc(s_x_in[j], 16)

        def sp_store_h(e, p, L, j):
            q = PASSES[p]
            e.wait_ge(s_mo, base(p, is_norm) + L + 1)
            e.dma_start(hT[q["layer"]][L], a_raw[:, j]).then_inc(s_hst[j], 16)

        def sp_store(e, p, L, j):
            q = PASSES[p]
            if keeps_T(q):
                dst, t0 = (kT1, 0) if q["name"] == "k1" else (qT1, 0)
                e.wait_ge(s_yTs, base(p, keeps_T) + L + 1)
                e.dma_start(dst.rearrange("h d (t p) -> t d h p", p=P)[L], yT[:, :, :]).then_inc(s_yst, 16)
                return
            e.wait_ge(s_y, base(p) + L + 1)
            y = y_out[:, j, :]
            if q["name"] == "v1":
                e.dma_start(v1.rearrange("h p t d -> t p h d")[L], y.rearrange("p (h d) -> p h d", h=AH))\
                    .then_inc(s_st[j], 16)
                return
            dst = {"qk0": qk0, "vg0": vg0}.get(q["name"])
            if dst is None:
                rows = {"pg0": pg0, "out0": x1, "g1": g1, "out1": out[0]}[q["name"]]
                dst = rows.rearrange("(t p) d -> t p d", p=P)
            e.dma_start(dst[L], y).then_inc(s_st[j], 16)

        def rope_w(q):
            return 2 * P if q["rope"] == 0 else 2 * DH

        def sp_pass(e, p):
            q = PASSES[p]
            nt = q["tiles"][1]
            if p and not early(p):
                if not ahead(p):
                    sp_load(e, p, 0, 0, 0, True)
                sp_load(e, p, 1, 0, 1, True)
            sp_late(e, p, 0, 0, 0, True)
            if is_norm(q):
                sp_store_h(e, p, 0, 0)

            def body(i, first, last):
                for j in range(2):
                    L = 2 * i + j
                    if j == 1 and p + 1 < NP_ and not (last and nt // 2 > KC):
                        sp_weights(e, p + 1, i)
                    if not last:
                        sp_load(e, p, L + 2, i + 1, j, False)
                    if is_norm(q) and not (last and j == 1):
                        sp_store_h(e, p, L + 1, 1 - j)
                    if last and early(p + 1):
                        sp_load(e, p + 1, j, 0, j, True)
                    if not (first and j == 0):
                        sp_store(e, p, L - 1, 1 - j)
                    if last and j == 1 and ahead(p + 1):
                        sp_load(e, p + 1, 0, 0, 0, True)
                    if not (last and j == 1):
                        sp_late(e, p, L + 1, i, 1 - j, first and j == 0)
                    if p == BACK:
                        if not (last and j == 1):
                            sp_back_load(e, i, j)
                        if not (first and j == 0):
                            sp_back_store(e, L - 1, 1 - j)

            pairs(e, p, body)
            sp_store(e, p, nt - 1, 1)
            if p == BACK:
                sp_back_store(e, nt - 1, 1)
                for s in s_b_st:
                    e.wait_ge(s, 8 * NT)


        def pool_settled(e):
            e.wait_ge(s_stage, 5)

        def pool_weights(e, p, i):
            s = p % 2
            e.wait_ge(s_w_in, 16 * (8 * p + i + 1))
            if p:
                pool_settled(e)
            e.tensor_copy(whi[s][:, i, :], w_raw[:, :]).then_inc(s_w_hi, 1)
            e.wait_ge(s_w_hi, 8 * p + i + 1)
            e.tensor_tensor(wlo[s][:, i, :], w_raw[:, :], whi[s][:, i, :], ALU.subtract)\
                .then_inc(s_w_split, 1)

        def pool_look(e, p, L, j):
            if not is_norm(PASSES[p]):
                return
            nn = base(p, is_norm) + L
            e.wait_ge(s_ss, nn + 1)
            e.tensor_tensor(ms[:, j], ss[:, j], eps_col[:, 0:1], ALU.add).then_inc(s_ms, 1)
            e.wait_ge(s_ms, nn + 1)
            e.tensor_tensor(rstd[:, j], ms[:, j], minus_half[:, 0:1], ALU.pow).then_inc(s_rstd, 1)

        def pool_main(e, p, L, i, j, first):
            q = PASSES[p]
            if first and j == 0 and p and (is_rope(q) or is_resid(q)):
                e.wait_ge(s_y, base(p))
            if is_rope(q):
                wait_y_out_free(e, p, L, i, j, first)
                e.wait_ge(s_tsin, base(p, is_rope) + L + 1)
                e.tensor_tensor(y_out[:, j, :], t_cos[:, :], t_sin[:, :], ALU.add).then_inc(s_y, 1)
            if is_resid(q):
                nr = base(p, is_resid) + L
                e.wait_ge(s_ss2, nr + 1)
                e.tensor_tensor(ms2[:, j], ss2[:, j], eps_col[:, 0:1], ALU.add).then_inc(s_ms2, 1)
                e.wait_ge(s_ms2, nr + 1)
                e.tensor_tensor(rstd2[:, j], ms2[:, j], minus_half[:, 0:1], ALU.pow).then_inc(s_rstd2, 1)
                wait_y_out_free(e, p, L, i, j, first)
                e.wait_ge(s_x_in[j], 16 * (base(p, has_x) // 2 + i + 1))
                e.wait_ge(s_res, nr + 1)
                e.tensor_tensor(y_out[:, j, :], t_sin[:, :], x_in[:, j, :], ALU.add).then_inc(s_y, 1)

        def pool_pass(e, p):
            nt = PASSES[p]["tiles"][1]
            if not ahead(p):
                pool_look(e, p, 0, 0)
            pool_look(e, p, 1, 1)
            if p > 0 and p + 1 < NP_:
                e.wait_ge(s_mm, 2 + base(p))

            def body(i, first, last):
                for j in range(2):
                    if not last:
                        pool_look(e, p, 2 * i + j + 2, j)
                    elif j == 1 and ahead(p + 1):
                        pool_look(e, p + 1, 0, 0)
                    pool_main(e, p, 2 * i + j, i, j, first)
                    if p == BACK and not (last and j == 1):
                        pool_back(e, i, j)
                if p + 1 < NP_ and not (last and nt // 2 > KC):
                    pool_weights(e, p + 1, i)

            pairs(e, p, body)


        def act_square(e, p, i, j):
            e.wait_ge(s_x_in[j], 16 * (base(p, has_x) // 2 + i + 1))
            e.activation(x_sq[:, :], x_in[:, j, :], ACT.Square, scale=D ** -0.5, accum_out=ss[:, j])\
                .then_inc(s_ss, 1)

        def act_norm(e, p, L, j):
            nn = base(p, is_norm) + L
            if not (isinstance(nn, int) and nn == 0):
                e.wait_ge(s_xT, nn)
            e.wait_ge(s_rstd, nn + 1)
            e.activation(x_n[:, :], x_in[:, j, :], ACT.Identity, scale=rstd[:, j]).then_inc(s_xn, 1)

        def act_look(e, p, L, i, j, more):
            if is_norm(PASSES[p]):
                act_norm(e, p, L, j)
                if more:
                    act_square(e, p, i + j, 1 - j)
            act_hi(e, p, L, i, j)

        def act_hi(e, p, L, i, j):
            if is_norm(PASSES[p]):
                e.wait_ge(s_mo, base(p, is_norm) + L + 1)
            else:
                e.wait_ge(s_a_in[j], 16 * (base(p, is_load) // 2 + i + 1))
            e.wait_ge(s_mm, base(p) + L + 1)
            e.activation(a_hi[j][:, :, :], a_raw[:, j], ACT.Copy).then_inc(s_hi, 1)

        def act_main(e, p, L, i, j, first):
            q = PASSES[p]
            y = y_ps[j].rearrange("p b n -> p (b n)")
            if keeps_T(q) and not (first and j == 0):
                act_yT(e, p, L - 1)
            if q["post"] == "gate":
                wait_y_out_free(e, p, L, i, j, first)
                e.wait_ge(s_mm, 2 + base(p) + L + 1)
                e.activation(y_out[:, j, HB:], y[:, HB:], ACT.Silu).then_inc(s_y2, 1)
            if q["post"] == "silu":
                e.wait_ge(s_y, base(p) + L)
                e.wait_ge(s_mm, 2 + base(p) + L + 1)
                e.activation(t_cos[:, :], y, ACT.Silu).then_inc(s_y2, 1)
            if is_resid(q):
                e.wait_ge(s_y, base(p) + L)
                e.wait_ge(s_mm, 2 + base(p) + L + 1)
                e.activation(t_cos[:, :], y, ACT.Square, scale=D ** -0.5, accum_out=ss2[:, j]).then_inc(s_ss2, 1)

        def act_yT(e, p, L):
            nT = base(p, keeps_T) + L
            if not (isinstance(nT, int) and nT == 0):
                e.wait_ge(s_yst, 16 * nT)
            e.wait_ge(s_yTp, nT + 1)
            factor = ASCALE if PASSES[p]["name"] == "q1" else 1.0
            e.activation(yT[:, :, :], tp_ps[1].rearrange("p b (k n) -> p (b k) n", n=P), ACT.Copy, scale=factor)\
                .then_inc(s_yTs, 1)

        def act_pass(e, p):
            nt = PASSES[p]["tiles"][1]
            if ahead(p):
                act_hi(e, p, 0, 0, 0)
                act_square(e, p, 0, 1)
            elif not early(p):
                if is_norm(PASSES[p]):
                    act_square(e, p, 0, 0)
                act_look(e, p, 0, 0, 0, True)

            def body(i, first, last):
                for j in range(2):
                    L = 2 * i + j
                    if not (last and j == 1):
                        act_look(e, p, L + 1, i + j, 1 - j, not last)
                    elif early(p + 1):
                        act_look(e, p + 1, 0, 0, 0, True)
                    elif ahead(p + 1):
                        act_square(e, p + 1, 0, 0)
                        act_norm(e, p + 1, 0, 0)
                    act_main(e, p, L, i, j, first)

            pairs(e, p, body)
            if keeps_T(PASSES[p]):
                act_yT(e, p, nt - 1)


        def dve_look(e, p, L, i, j, stream):
            q = PASSES[p]
            if is_norm(q):
                nn = base(p, is_norm) + L
                l = q["layer"]
                if not (isinstance(nn, int) and nn < 2):
                    e.wait_ge(s_hst[j], 16 * (base(p, is_norm) // 2 + i))
                e.wait_ge(s_xT, nn + 1)
                xT = tp_ps[0].rearrange("p b (k n) -> p (b k) n", n=P)
                for k in range(KC):
                    last = e.tensor_scalar(a_raw[:, j, k, :], xT[:, k, :], scale[:, l, k, stream:stream + 1],
                                           shift[:, l, k, stream:stream + 1], ALU.mult, ALU.add)
                last.then_inc(s_mo, 1)
            e.wait_ge(s_hi, base(p) + L + 1)
            e.tensor_tensor(a_lo[j][:, :, :], a_raw[:, j], a_hi[j][:, :, :], ALU.subtract).then_inc(s_split, 1)

        def dve_main(e, p, L, i, j, first):
            q = PASSES[p]
            if first and j == 0 and q["post"] in ("gate", "copy", "silu"):
                e.wait_ge(s_y, base(p))
            y = y_ps[j].rearrange("p b n -> p (b n)")
            if is_rope(q):
                hd = rope_w(q) // 2
                e.wait_ge(s_rope_in[j], 16 * (base(p, is_rope) // 2 + i + 1))
                if not (isinstance(L, int) and L + base(p) == 0):
                    e.wait_ge(s_y, base(p) + L)
                e.wait_ge(s_mm, 2 + base(p) + L + 1)
                c = rope_in[:, j, 0:hd].unsqueeze(1).to_broadcast([P, D // hd, hd])
                e.tensor_tensor(t_cos.rearrange("p (h d) -> p h d", d=hd), y.rearrange("p (h d) -> p h d", d=hd),
                                c, ALU.mult)
                s = rope_in[:, j, hd:2 * hd].rearrange("p (a b d) -> p a b d", a=2, b=2)
                yv = y.rearrange("p (h a b d) -> p h a b d", a=2, b=2, d=hd // 4)
                tv = t_sin.rearrange("p (h a b d) -> p h a b d", a=2, b=2, d=hd // 4)
                for b in range(2):
                    sv = s[:, :, b, :].unsqueeze(1).to_broadcast([P, D // hd, 2, hd // 4])
                    last = e.tensor_tensor(tv[:, :, :, b, :], yv[:, :, :, 1 - b, :], sv, ALU.mult)
                last.then_inc(s_tsin, 1)
            if q["post"] in ("gate", "copy"):
                w = HB if q["post"] == "gate" else D
                wait_y_out_free(e, p, L, i, j, first)
                if q["post"] == "gate":
                    e.wait_ge(s_y2, base(p, act_reads) + L + 1)
                e.wait_ge(s_mm, 2 + base(p) + L + 1)
                e.tensor_copy(y_out[:, j, 0:w], y[:, 0:w]).then_inc(s_y, 1)
            if q["post"] == "silu":
                wait_y_out_free(e, p, L, i, j, first)
                e.wait_ge(s_y2, base(p, act_reads) + L + 1)
                e.tensor_tensor(y_out[:, j, :].rearrange("p (h d) -> p h d", d=P),
                                t_cos.rearrange("p (h d) -> p h d", d=P),
                                subln[:, 1:2, :].to_broadcast([P, AH, P]), ALU.mult).then_inc(s_y, 1)
            if is_resid(q):
                g = 2 if q["layer"] else 0 if first else 1
                e.wait_ge(s_y, base(p) + L)
                e.wait_ge(s_rstd2, base(p, is_resid) + L + 1)
                e.scalar_tensor_tensor(out=t_sin[:, :], in0=y, scalar=rstd2[:, j], in1=gate_post[:, g, :],
                                       op0=ALU.mult, op1=ALU.mult).then_inc(s_res, 1)

        def dve_pass(e, p):
            ctx_first = PASSES[p]["tiles"][0] == 0
            if not early(p) and not ahead(p):
                dve_look(e, p, 0, 0, 0, 0)

            def body(i, first, last):
                for j in range(2):
                    L = 2 * i + j
                    if not (last and j == 1):
                        dve_look(e, p, L + 1, i + j, 1 - j, 0 if first and j == 0 else 1)
                    elif early(p + 1) or ahead(p + 1):
                        dve_look(e, p + 1, 0, 0, 0, 0)
                    if p == BACK and not (first and j == 0):
                        dve_back(e, L - 1, 1 - j)
                    dve_main(e, p, L, i, j, first)

            if p == BACK:
                e.wait_ge(s_xn, base(p, is_norm))
                e.memset(x_sq[:, 0:HB], 0.0).then_inc(s_b_S, 1)
            pairs(e, p, body)


        def pe_xT(e, p, L):
            nn = base(p, is_norm) + L
            if not (isinstance(nn, int) and nn == 0):
                e.wait_ge(s_mo, nn)
            e.wait_ge(s_xn, nn + 1)
            xT = tp_ps[0].rearrange("p b (k n) -> p (b k) n", n=P)
            for k in range(KC):
                last = e.transpose(xT[:, k, :], x_n[:, k * P:(k + 1) * P], ident[:, :])
            last.then_inc(s_xT, 1)

        def pe_yT(e, p, L, j):
            nT = base(p, keeps_T) + L
            if not (isinstance(nT, int) and nT == 0):
                e.wait_ge(s_yTs, nT)
            e.wait_ge(s_y, base(p) + L + 1)
            y = tp_ps[1].rearrange("p b (k n) -> p (b k) n", n=P)
            for k in range(KC):
                last = e.transpose(y[:, k, :], y_out[:, j, k * P:(k + 1) * P], ident[:, :])
            last.then_inc(s_yTp, 1)

        def pe_tile(e, p, L, j, first, last_tile):
            q = PASSES[p]
            wait_y_ps_free(e, p, L, first)
            e.wait_ge(s_split, 2 + base(p) + L + 1)
            hi, lo = whi[p % 2], wlo[p % 2]
            for k in range(KC):
                for a, w in ((a_hi[j], hi), (a_hi[j], lo), (a_lo[j], hi)):
                    for b in range(2):
                        mm = e.matmul(y_ps[j][:, b, :], a[:, k, :], w[:, k, b * HB:(b + 1) * HB],
                                      start=(k == 0 and a is a_hi[j] and w is hi),
                                      stop=(k == KC - 1 and a is a_lo[j]))
                if k == 4 and keeps_T(q) and not (first and j == 0):
                    pe_yT(e, p, L - 1, 1 - j)
                if k == 1 and is_norm(q) and not last_tile:
                    pe_xT(e, p, L + 1)
                if k == 3 and p == BACK and not (first and j == 0):
                    pe_back(e, L - 1, 1 - j)
            mm.then_inc(s_mm, 1)

        def pe_pass(e, p):
            nt = PASSES[p]["tiles"][1]
            if is_norm(PASSES[p]):
                pe_xT(e, p, 0)
            e.wait_ge(s_w_split, 8 * (p + 1))

            def body(i, first, last):
                for j in range(2):
                    pe_tile(e, p, 2 * i + j, j, first, last and j == 1)

            pairs(e, p, body)
            if keeps_T(PASSES[p]):
                pe_yT(e, p, nt - 1, 1)


        s_rc = sem("s_rc")
        s_rp = sem("s_rp")
        s_rv = sem("s_rv")
        s_ra = sem("s_ra")
        s_qk_in = [sem(f"s_qk_in{j}") for j in range(2)]
        s_pg_in = [sem(f"s_pg_in{j}") for j in range(2)]
        s_vr_in = [sem(f"s_vr_in{j}") for j in range(2)]
        s_gr_in = [sem(f"s_gr_in{j}") for j in range(2)]
        s_bs_in = [sem(f"s_bs_in{j}") for j in range(2)]
        s_f_T = sem("s_f_T")
        s_f_qkT = sem("s_f_qkT")
        s_f_qd = sem("s_f_qd")
        s_f_dT = sem("s_f_dT")
        s_f_pT = sem("s_f_pT")
        s_f_k = sem("s_f_k")
        s_f_g = sem("s_f_g")
        s_f_U = sem("s_f_U")
        s_f_S = sem("s_f_S")
        s_f_sc = sem("s_f_sc")
        s_f_scm = sem("s_f_scm")
        s_f_yp = sem("s_f_yp")
        s_f_o = sem("s_f_o")
        s_f_sum = sem("s_f_sum")
        s_f_oc = sem("s_f_oc")
        s_f_sq = sem("s_f_sq")
        s_f_var = sem("s_f_var")
        s_f_ve = sem("s_f_ve")
        s_f_rs = sem("s_f_rs")
        s_f_on = sem("s_f_on")
        s_f_mixr = sem("s_f_mixr")
        s_f_mixp = sem("s_f_mixp")
        s_f_rTT = sem("s_f_rTT")
        s_f_pTT = sem("s_f_pTT")
        s_f_rTs = sem("s_f_rTs")
        s_f_pTs = sem("s_f_pTs")
        s_held_r = sem("s_held_r")
        s_f_rst = sem("s_f_rst")
        s_f_pst = sem("s_f_pst")

        qkT_ps = ps[:, 0:2, :].rearrange("p a (h n) -> p a h n", n=P)
        sc_ps, o_ps, U_ps, dT_ps, yp_ps, fT_ps = [ps[:, b, :].rearrange("p (h n) -> p h n", n=P) for b in range(2, 8)]
        def chunk_runs(e, body):
            for a, v in enumerate((1, 2, 1, 0)):
                body(a, a % 2, v)
            with e.Fori(2, NT // 2 - 2) as i:
                for j in range(2):
                    body(2 * i + j, j, 0)
            for a, v in ((NT - 4, 0), (NT - 3, 0), (NT - 2, 0), (NT - 1, 2), (NT, 0), (NT + 1, 0)):
                body(a, a % 2, v)

        def sp_ret(e):
            blocks = pg0.rearrange("(n r) d -> n r d", r=HALO)
            per = P // HALO

            def load_qk(c, j):
                e.dma_start(qk_in[:, j, :], qk0[c]).then_inc(s_qk_in[j], 16)

            def load_pg(c, j):
                e.dma_start(pg_in[:, j, :], pg0.rearrange("(t p) d -> t p d", p=P)[c]).then_inc(s_pg_in[j], 16)
                before = per * c - 1 if has(c, 1, NT) else 0
                behind = per * c + per if has(c, 0, NT - 1) else NT * per - 1
                e.dma_start(halo_in[0:HALO, j, :], blocks[before, :, 0:HB]).then_inc(s_pg_in[j], 16)
                e.dma_start(halo_in[HALO:2 * HALO, j, :], blocks[behind, :, 0:HB]).then_inc(s_pg_in[j], 16)

            def load_v(c, j):
                e.dma_start(vg_in[:, j, 0:HB], vg0[c, :, 0:HB]).then_inc(s_vr_in[j], 16)
                step = 1 - c if isinstance(c, int) and c < 2 else (-1) * c + (NT + 1)
                e.dma_start(back_in[:, j], back_st[step]).then_inc(s_bs_in[j], 16)

            e.dma_start(rel[:, :, :], A["rel"]).then_inc(s_rc, 16)
            e.dma_start(dec_rows[:, :, :], A["dec_rows"]).then_inc(s_rc, 16)
            load_qk(0, 0)
            e.dma_start(pool_own[:, :, :, :], A["pool_own"]).then_inc(s_rp, 16)
            e.dma_start(pool_halo[:, :, :, :], A["pool_halo"]).then_inc(s_rp, 16)
            load_pg(0, 0)
            e.dma_start(pool_w[:, :, :], A["pool_w"][0].rearrange("g c d -> c g d")).then_inc(s_rp, 16)
            e.dma_start(pool_scale[:, :], row_broadcast(A["pool_scale"][0])).then_inc(s_rp, 16)
            load_v(0, 0)
            load_qk(1, 1)
            load_pg(1, 1)

            def body(a, j, v):
                if has(a, 1, NT + 1):
                    e.wait_ge(s_f_pTs, a)
                    e.sem_inc(s_held_r, 1)
                    e.dma_start(mixT[a - 1][:, RH:, :], mixT_s[:, RH:, :]).then_inc(s_f_pst, 16)
                if has(a, 0, NT - 2):
                    e.wait_ge(s_f_T, a + 1)
                    e.wait_ge(s_f_k, a + 1)
                    load_qk(a + 2, j)
                    e.wait_ge(s_f_dT, a + 1)
                    e.wait_ge(s_f_g, a + 1)
                    load_pg(a + 2, j)
                if has(a, 0, NT):
                    if has(a, 2, NT):
                        e.wait_ge(s_f_mixr, a - 1)
                    e.dma_start(vg_in[:, j, HB:], vg0[a, :, HB:]).then_inc(s_gr_in[j], 16)
                if has(a, 0, NT - 1):
                    ge(e, s_f_o, a)
                    e.sem_inc(s_held_r, 1)
                    load_v(a + 1, 1 - j)
                if has(a, 2, NT + 2):
                    e.wait_ge(s_f_rTs, a - 1)
                    e.sem_inc(s_held_r, 1)
                    e.dma_start(mixT[a - 2][:, 0:RH, :], mixT_s[:, 0:RH, :]).then_inc(s_f_rst, 16)

            chunk_runs(e, body)
            e.wait_ge(s_f_rst, 16 * NT)
            e.wait_ge(s_f_pst, 16 * NT)

        def act_ret(e):
            e.wait_ge(s_rc, 32)
            for d in range(2):
                for h in range(RH):
                    e.activation(e_rel[:, d, h, :], rel[:, d, :], ACT.Exp, scale=log_g[:, d, h:h + 1])
                    ins = e.activation(q_dec[:, d, h, :], dec_rows[:, d, :], ACT.Exp, scale=log_g[:, d, h:h + 1])
            ins.then_inc(s_ra, 1)

            def body(a, j, v):
                if has(a, 0, NT):
                    ge(e, s_f_sc, a)
                    ge(e, s_f_qd, a)
                    e.wait_ge(s_f_T, a + 1)
                    e.activation(qkT[:, :, :, :], qkT_ps, ACT.Copy).then_inc(s_f_qkT, 1)
                if has(a, 2, NT + 2):
                    e.wait_ge(s_f_oc, a - 1)
                    e.activation(o_sq[:, :, :], o_cent[:, :, :], ACT.Square, scale=P ** -0.5).then_inc(s_f_sq, 1)
                if has(a, 1, NT + 1):
                    ge(e, s_f_pst, 16 * (a - 1))
                    e.wait_ge(s_f_pTT, a)
                    e.activation(mixT_s[:, RH:, :], fT_ps, ACT.Copy).then_inc(s_f_pTs, 1)
                if has(a, 0, NT):
                    ge(e, s_f_yp, a)
                    e.wait_ge(s_f_dT, a + 1)
                    e.activation(poolT[:, :, :], dT_ps, ACT.Copy).then_inc(s_f_pT, 1)
                if has(a, 2, NT + 2):
                    ge(e, s_f_rst, 16 * (a - 2) if has(a, 3, NT + 2) else 0)
                    e.wait_ge(s_f_rTT, a - 1)
                    e.activation(mixT_s[:, 0:RH, :], fT_ps, ACT.Copy).then_inc(s_f_rTs, 1)

            chunk_runs(e, body)

        def dve_ret(e):
            n = 0

            def step(ins):
                nonlocal n
                n += 1
                ins.then_inc(s_rv, 1)
                e.wait_ge(s_rv, n)

            e.wait_ge(s_ra, 1)
            e.wait_ge(s_rc, 32)
            for d, dst in ((0, decay_mask), (1, mask_b)):
                step(e.tensor_tensor(dst[:, :, :], e_rel[:, d], rel[:, 2 + d:3 + d, :].to_broadcast([P, RH, P]),
                                     ALU.mult))
            step(e.tensor_tensor(decay_mask[:, :, :], decay_mask[:, :, :], mask_b[:, :, :], ALU.add))
            e.memset(fwd_state[:, 0], 0.0).then_inc(s_f_S, 1)

            def body(a, j, v):
                if has(a, 2, NT + 2):
                    e.wait_ge(s_f_o, a - 1)
                    e.tensor_reduce(head_sum[:, :], o_ps, AX.X, ALU.add).then_inc(s_f_sum, 1)
                    e.wait_ge(s_f_sum, 2 * a - 3)
                    e.tensor_scalar(head_mean[:, :], head_sum[:, :], -1.0 / P, None, ALU.mult).then_inc(s_f_sum, 1)
                    e.wait_ge(s_f_sum, 2 * a - 2)
                    e.tensor_tensor(o_cent[:, :, :], o_ps, heads(head_mean[:, :]), ALU.add).then_inc(s_f_oc, 1)
                if has(a, 1, NT):
                    e.wait_ge(s_f_S, a)
                    e.wait_ge(s_f_U, a)
                    for h in range(RH):
                        ins = e.scalar_tensor_tensor(out=fwd_state[:, j, h, :], in0=fwd_state[:, 1 - j, h, :],
                                                     scalar=c_dec[:, 0, h:h + 1], in1=U_ps[:, h, :],
                                                     op0=ALU.mult, op1=ALU.add)
                    ins.then_inc(s_f_S, 1)
                if has(a, 0, NT):
                    e.wait_ge(s_f_qkT, a + 1)
                    for d in range(2):
                        ins = e.tensor_tensor(qT_dec[:, j, d], qkT[:, 0], q_dec[:, d], ALU.mult)
                    ins.then_inc(s_f_qd, 1)
                if has(a, 2, NT + 2):
                    e.wait_ge(s_f_sq, a - 1)
                    e.tensor_reduce(head_var[:, :], o_sq[:, :, :], AX.X, ALU.add).then_inc(s_f_var, 1)
                if has(a, 0, NT):
                    e.wait_ge(s_f_sc, a + 1)
                    e.tensor_tensor(sc_masked[:, j], sc_ps, decay_mask[:, :, :], ALU.mult).then_inc(s_f_scm, 1)
                if has(a, 2, NT + 2):
                    e.wait_ge(s_f_rs, a - 1)
                    e.tensor_tensor(o_norm[:, :, :], o_cent[:, :, :], heads(head_rstd[:, :]), ALU.mult)\
                        .then_inc(s_f_on, 1)
                    e.wait_ge(s_gr_in[j], 8 * (a - j))
                    ge(e, s_f_rTT, a - 2 if has(a, 3, NT + 2) else 0)
                    e.wait_ge(s_f_on, a - 1)
                    e.tensor_tensor(mix[:, 0:RH, :], o_norm[:, :, :],
                                    vg_in[:, j, HB:].rearrange("p (h n) -> p h n", n=P), ALU.mult)\
                        .then_inc(s_f_mixr, 1)
                if has(a, 0, NT):
                    ge(e, s_f_pTT, a)
                    e.wait_ge(s_f_g, a + 1)
                    e.wait_ge(s_f_yp, a + 1)
                    e.tensor_tensor(mix[:, RH:, :], yp_ps, gate_scaled.rearrange("p (h n) -> p h n", n=P), ALU.mult)\
                        .then_inc(s_f_mixp, 1)

            chunk_runs(e, body)

        def pool_ret(e):
            def body(a, j, v):
                if has(a, 0, NT):
                    if has(a, 2, NT):
                        e.wait_ge(s_f_U, a - 1)
                    e.wait_ge(s_qk_in[j], 8 * (a - j) + 16)
                    e.tensor_tensor(k_scaled[:, j], qk_in[:, j, HB:].rearrange("p (h n) -> p h n", n=P),
                                    heads(k_dec[:, 0, :]), ALU.mult).then_inc(s_f_k, 1)
                    if not has(a, 1, NT):
                        e.wait_ge(s_rp, 64)
                    ge(e, s_f_mixp, a)
                    e.wait_ge(s_pg_in[j], 24 * (a - j) + 48)
                    e.tensor_tensor(gate_scaled[:, :], pg_in[:, j, HB:], pool_scale[:, :], ALU.mult).then_inc(s_f_g, 1)
                if has(a, 2, NT + 2):
                    e.wait_ge(s_f_var, a - 1)
                    e.tensor_tensor(head_var2[:, :], head_var[:, :], eps_col[:, :], ALU.add).then_inc(s_f_ve, 1)
                    e.wait_ge(s_f_ve, a - 1)
                    e.tensor_tensor(head_rstd[:, :], head_var2[:, :], minus_half[:, :], ALU.pow).then_inc(s_f_rs, 1)

            chunk_runs(e, body)

        def pe_ret(e):
            def turn_mix(half, done):
                for h in range(RH):
                    t = e.transpose(fT_ps[:, h, :], mix[:, half + h, :], ident[:, :])
                t.then_inc(done, 1)

            def body(a, j, v):
                if has(a, 0, NT):
                    e.wait_ge(s_qk_in[j], 8 * (a - j) + 16)
                    ge(e, s_f_qkT, a)
                    for b in range(2):
                        for h in range(RH):
                            t = e.transpose(qkT_ps[:, b, h, :], qk_in[:, j, (RH * b + h) * P:(RH * b + h + 1) * P],
                                            ident[:, :])
                    t.then_inc(s_f_T, 1)
                if has(a, 1, NT + 1):
                    if has(a, 3, NT + 1):
                        e.wait_ge(s_f_rTs, a - 2)
                    ge(e, s_f_pTs, a - 1)
                    e.wait_ge(s_f_mixp, a)
                    turn_mix(RH, s_f_pTT)
                if has(a, 0, NT):
                    e.wait_ge(s_pg_in[j], 24 * (a - j) + 48)
                    if not has(a, 1, NT):
                        e.wait_ge(s_rp, 64)
                    ge(e, s_f_pT, a)
                    for g in range(PG):
                        e.matmul(dT_ps[:, g, :], pg_in[:, j, g * P:(g + 1) * P], pool_own[:, v, g, :],
                                 start=True, stop=False)
                        mm = e.matmul(dT_ps[:, g, :], halo_in[:, j, g * P:(g + 1) * P], pool_halo[:, v, g, :],
                                      start=False, stop=True)
                    mm.then_inc(s_f_dT, 1)
                    ge(e, s_f_scm, a)
                    e.wait_ge(s_f_qkT, a + 1)
                    for h in range(RH):
                        mm = e.matmul(sc_ps[:, h, :], qkT[:, 1, h, :], qkT[:, 0, h, :], start=True, stop=True)
                    mm.then_inc(s_f_sc, 1)
                    ge(e, s_f_mixp, a)
                    e.wait_ge(s_f_pT, a + 1)
                    for g in range(PG):
                        mm = e.matmul(yp_ps[:, g, :], poolT[:, g, :], pool_w[:, g, :], start=True, stop=True)
                    mm.then_inc(s_f_yp, 1)
                    e.wait_ge(s_f_S, a + 1)
                    e.wait_ge(s_f_k, a + 1)
                    e.wait_ge(s_vr_in[j], 8 * (a - j) + 16)
                    for h in range(RH):
                        mm = e.matmul(U_ps[:, h, :], k_scaled[:, j, h, :], vg_in[:, j, h * P:(h + 1) * P],
                                      start=True, stop=True)
                    mm.then_inc(s_f_U, 1)
                if has(a, 1, NT + 1):
                    i = 1 - j
                    e.wait_ge(s_bs_in[i], 8 * (a - 1 - i) + 16)
                    if has(a, 2, NT + 1):
                        e.wait_ge(s_f_oc, a - 1)
                    e.wait_ge(s_f_qd, a)
                    e.wait_ge(s_f_scm, a)
                    e.wait_ge(s_f_S, a)
                    for h in range(RH):
                        e.matmul(o_ps[:, h, :], sc_masked[:, i, h, :], vg_in[:, i, h * P:(h + 1) * P],
                                 start=True, stop=False)
                        e.matmul(o_ps[:, h, :], qT_dec[:, i, 0, h, :], fwd_state[:, i, h, :], start=False, stop=False)
                        mm = e.matmul(o_ps[:, h, :], qT_dec[:, i, 1, h, :], back_in[:, i, h, :],
                                      start=False, stop=True)
                    mm.then_inc(s_f_o, 1)
                if has(a, 2, NT + 2):
                    e.wait_ge(s_f_pTs, a if has(a, 0, NT) else NT)
                    e.wait_ge(s_f_mixr, a - 1)
                    turn_mix(0, s_f_rTT)

            chunk_runs(e, body)


        NU = AH * LT
        S_COLS = [(c * HB, min(T, (c + 1) * HB)) for c in range((T + HB - 1) // HB)]
        PARTS = [(0, 2 * HB), (2 * HB, 3 * HB), (3 * HB, T)]
        NPART = len(PARTS)
        GROUPS = [range(4 * g, min(NT, 4 * g + 4)) for g in range((NT + 3) // 4)]
        NG = len(GROUPS)
        TORD = {0: 0, 1: 1, 2: 2, 3: 3, 4: 4, "o": 5}
        PT_SLOT = (0, 1, 2, 0, 1)
        CUT = 3 * HB
        NTO = len(TORD)

        s_q_in = [sem(f"s_q_in{j}") for j in range(2)]
        s_k_in = [sem(f"s_k_in{j}") for j in range(2)]
        s_v_in = [sem(f"s_v_in{j}") for j in range(2)]
        s_g_in = [sem(f"s_g_in{j}") for j in range(2)]
        s_held = sem("s_held")
        s_qh = sem("s_qh")
        s_qs = sem("s_qs")
        s_kh = sem("s_kh")
        s_ks = sem("s_ks")
        s_S = sem("s_S")
        s_mx = sem("s_mx")
        s_nb = sem("s_nb")
        s_exp = sem("s_exp")
        s_c = sem("s_c")
        s_comb = sem("s_comb")
        s_comb_p = sem("s_comb_p")
        s_scaled = sem("s_scaled")
        s_T = sem("s_T")
        s_Te = sem("s_Te")
        s_pv = sem("s_pv")
        s_o1 = sem("s_o1")
        s_osq = sem("s_osq")
        s_oms = sem("s_oms")
        s_ors = sem("s_ors")
        s_og = sem("s_og")
        s_ost = [sem(f"s_ost{j}") for j in range(2)]

        S_ps = ps[:, 0:5, :].rearrange("p b n -> p (b n)")
        T_ps = [ps[:, 5 + b, :].rearrange("p (k n) -> p k n", n=P) for b in range(2)]
        O_ps = ps[:, 7, 0:P]
        K0_PARTS = 4
        K0 = T // K0_PARTS
        s_k0_in = [sem(f"s_k0_in{c}") for c in range(K0_PARTS)]
        k0_raw = prob[:, 0:2, :]
        k_hi_s = k_hi.rearrange("p a m (s c) -> p a s m c", c=KS)
        k_lo_s = k_lo.rearrange("p a m (s c) -> p a s m c", c=KS)
        v_in_s = v_in.rearrange("p a t d -> p a (t d)").rearrange("p a (s c) -> p a s c", c=NT * P // LT)
        kT1_s = kT1.rearrange("h (m d) (s c) -> h s d m c", m=2, c=KS)
        qT1_s = qT1.rearrange("h (m d) (t n) -> h t d m n", m=2, n=P)
        v1_s = v1.rearrange("h p t d -> h p (t d)").rearrange("h p (s c) -> h s p c", c=NT * P // LT)
        g1_s = g1.rearrange("(t p) (h d) -> h t p d", p=P, d=P)
        oT1_s = oT1.rearrange("h d (t n) -> h t d n", n=P)

        def head_tile(e, u):
            if isinstance(u, int):
                return u // LT, u % LT
            h = nc.s_assert_within(u >> 4, 0, AH - 1,
                                   skip_runtime_bounds_check_because="tiles are numbered below AH * LT")
            return h, u & (LT - 1)

        def place(w, g):
            return NTO * w + (0 if isinstance(w, int) and w == NU else TORD[g])

        def bank(w, g):
            return 0 if isinstance(w, int) and w == NU else TORD[g] % 2

        def parity(h):
            return h & 1

        def steps(e, body, cuts=()):
            for u in range(2):
                body(u, u, u)
            edges = [1, 2, *cuts, NU // 2]
            for a, b in zip(edges, edges[1:]):
                if b - a == 1:
                    for j in range(2):
                        body(2 * a + j, j, 2 * a + j)
                else:
                    with e.Fori(a, b) as i:
                        for j in range(2):
                            body(2 * i + j, j, 2 * (b - 1) + j)
            for j in range(2):
                body(NU + j, j, NU + j)

        def sp_att(e):
            def hold(s, v):
                ge(e, s, v)
                e.sem_inc(s_held, 1)

            def q(u, j, wait):
                h, t = head_tile(e, u)
                if wait:
                    hold(s_qs, u - 1)
                for d in range(2):
                    e.dma_start(q_raw[d * DH:(d + 1) * DH, j], qT1_s[h, t]).then_inc(s_q_in[j], 16)

            def k(n, j, wait):
                h, s = head_tile(e, n)
                if wait:
                    hold(s_ks, n - 1)
                for d in range(2):
                    e.dma_start(k_raw[d * DH:(d + 1) * DH, j], kT1_s[h, s]).then_inc(s_k_in[j], 16)

            def v(n, j, step=None):
                h, s = head_tile(e, n)
                if step is not None:
                    hold(s_pv, NG * (step - 2))
                e.dma_start(v_in_s[:, parity(h), s], v1_s[h, s]).then_inc(s_v_in[j], 16)

            for c in range(K0_PARTS):
                cols = slice(c * K0, (c + 1) * K0)
                for d in range(2):
                    e.dma_start(k0_raw[d * DH:(d + 1) * DH, :, cols],
                                kT1.rearrange("h (m d) t -> h d m t", m=2)[0, :, :, cols]).then_inc(s_k0_in[c], 16)
                if c < 2:
                    q(c, c, False)
            for n in range(LT, LT + 2):
                k(n, n % 2, False)
            for n in range(LT):
                v(n, n % 2)

            def body(u, j, top):
                if top + 2 < NU:
                    q(u + 2, j, True)
                if top < NU:
                    h, t = head_tile(e, u)
                    if has(u, 2, NU):
                        hold(s_og, u - 1)
                    e.dma_start(g_in[:, j, :], g1_s[h, t]).then_inc(s_g_in[j], 16)
                if j == 0 and has(u, 2, NU) and top + LT - 1 < NU:
                    for b in range(2):
                        v(u + (LT - 2 + b), b, u)
                if top + LT + 2 < NU:
                    k(u + LT + 2, j, True)
                if has(u, 3, NU + 2):
                    store(u - 3, 1 - j)

            def store(w, j):
                h, t = head_tile(e, w)
                hold(s_Te, place(w + 1, "o") + 1)
                e.dma_start(oT1_s[h, t], oT_s[:, j, :]).then_inc(s_ost[j], 16)

            steps(e, body, cuts=((NU - LT - 2) // 2, (NU - LT + 2) // 2, NU // 2 - 1))
            store(NU - 1, 1)
            for s in s_ost:
                e.wait_ge(s, 8 * NU)

        def pool_att(e):
            def zeros(n):
                return zero_col[:, :].unsqueeze(2).to_broadcast([P, 2, n])

            def n_is_late(n):
                return not isinstance(n, int) or n >= 2 * LT

            def split_k(n, j):
                h, s = head_tile(e, n)
                dst = (k_hi_s[:, parity(h), s], k_lo_s[:, parity(h), s])
                if n_is_late(n):
                    e.wait_ge(s_S, 2 * NPART * (n - LT))
                e.wait_ge(s_k_in[j], 16 * (n - LT - j) + 32)
                e.tensor_tensor(dst[0], k_raw[:, j], zeros(KS), ALU.add).then_inc(s_kh, 1)
                e.wait_ge(s_kh, n + 1)
                e.tensor_tensor(dst[1], k_raw[:, j], dst[0], ALU.subtract).then_inc(s_ks, 1)

            def split_q(u, j):
                if has(u, 2, NU):
                    e.wait_ge(s_S, 2 * NPART * (u - 1))
                e.wait_ge(s_q_in[j], 16 * (u - j) + 32)
                e.tensor_tensor(q_st[j][:, :, :], q_raw[:, j], zeros(P), ALU.add).then_inc(s_qh, 1)
                e.wait_ge(s_qh, u + 1)
                low = slice(DH, P)
                e.tensor_tensor(q_st[j][low], q_raw[low, j], q_st[j][low], ALU.subtract).then_inc(s_qs, 1)
                e.wait_ge(s_qs, u + 1)

            split_q(0, 0)

            def ratios(u, j):
                e.wait_ge(s_exp, NPART * (2 * u + 2))
                e.tensor_tensor(den_part[:, :], sums[:, j, :, 0], sums[:, j, :, 1], ALU.add).then_inc(s_c, 1)
                e.wait_ge(s_c, 5 * u + 1)
                e.tensor_tensor(denom[:, :], den_part[:, :], sums[:, j, :, 2], ALU.add).then_inc(s_c, 1)
                e.wait_ge(s_c, 5 * u + 2)
                e.tensor_tensor(rden[:, j, :], denom[:, :], minus_one[:, :], ALU.pow).then_inc(s_c, 1)
                e.tensor_tensor(lam_den[:, :], denom[:, 0:1], neg_lam[:, 0:1], ALU.mult).then_inc(s_c, 1)
                e.wait_ge(s_c, 5 * u + 4)
                e.tensor_tensor(ratio[:, j, :], lam_den[:, :], rden[:, j, 1:2], ALU.mult).then_inc(s_c, 1)

            def body(u, j, top):
                if has(u, 1, NU + 1):
                    ratios(u - 1, 1 - j)
                    e.wait_ge(s_c, 5 * u)
                    e.tensor_tensor(prob[:, 2, CUT:], prob[:, 2, CUT:], ratio[:, 1 - j, :].to_broadcast([P, T - CUT]),
                                    ALU.mult).then_inc(s_scaled, 1)
                    e.wait_ge(s_scaled, u)
                    e.tensor_tensor(prob[:, 1 - j, CUT:], prob[:, 2, CUT:], prob[:, 1 - j, CUT:], ALU.add)\
                        .then_inc(s_comb_p, 1)
                if top + 1 < NU:
                    split_q(u + 1, 1 - j)
                if has(u, 2, NU + 2):
                    e.wait_ge(s_osq, u - 1)
                    e.tensor_tensor(o_ms[:, j], o_ss[:, j], eps_col[:, 0:1], ALU.add).then_inc(s_oms, 1)
                    e.wait_ge(s_oms, u - 1)
                    e.tensor_tensor(o_rstd[:, j], o_ms[:, j], minus_half[:, 0:1], ALU.pow).then_inc(s_ors, 1)
                if top + LT < NU:
                    split_k(u + LT, j)

            steps(e, body, cuts=((NU - LT) // 2, NU // 2 - 1))

        def pe_att(e):
            def scores(u, j, m, between):
                h, _ = head_tile(e, u)
                if m == 0:
                    e.wait_ge(s_qs, u + 1)
                    if has(u, 1, NU):
                        e.wait_ge(s_ks, LT * (h + 1))
                for c, (a, b) in enumerate(S_COLS):
                    if not has(u, 1, NU) and m == 0:
                        e.wait_ge(s_ks, LT // K0_PARTS * ((b + K0 - 1) // K0))
                    if c in between:
                        between[c]()
                    if c in (0, 2, 3):
                        ge(e, s_exp, NPART * (2 * u + m - 1) + (0, 0, 1, 2)[c] + 1 if has(u, 1, NU) or m else 0)
                    out_ = S_ps[:, a:b]
                    e.matmul(out_, q_st[j][:, m, :], k_hi[:, parity(h), m, a:b], start=True, stop=False)
                    mm = e.matmul(out_, q_st[j][:, m, :], k_lo[:, parity(h), m, a:b], start=False, stop=True)
                    if c in (1, 2, 4):
                        mm.then_inc(s_S, 1)

            def turn(w, j, g):
                x = place(w, g)
                if g == 0:
                    e.wait_ge(s_comb, w + 1)
                if g == 3:
                    e.wait_ge(s_comb_p, w + 1)
                if g == "o":
                    if has(w, 1, NU + 1):
                        e.wait_ge(s_og, w)
                    else:
                        e.wait_ge(s_rv, 4)
                ge(e, s_Te, x - 1)
                dst = T_ps[bank(w, g)]
                if g == "o":
                    t = e.transpose(dst[:, 0, :], o_gated[:, 1 - j, :], ident[:, :])
                else:
                    for b, kt in enumerate(GROUPS[g]):
                        t = e.transpose(dst[:, b, :], prob[:, j, kt * P:(kt + 1) * P], ident[:, :])
                t.then_inc(s_T, 1)

            def times_v(w, j, g):
                h, _ = head_tile(e, w)
                if g == 0:
                    for s in s_v_in:
                        e.wait_ge(s, 8 * LT * (h + 1))
                    ge(e, s_o1, w)
                e.wait_ge(s_Te, NTO * w + TORD[g] + 1)
                for b, kt in enumerate(GROUPS[g]):
                    mm = e.matmul(O_ps, probT[:, PT_SLOT[g], b, :], v_in[:, parity(h), kt, :],
                                  start=(kt == 0), stop=(kt == NT - 1))
                mm.then_inc(s_pv, 1)

            def body(u, j, top):
                old, new = has(u, 2, NU + 2), has(u, 1, NU + 1)

                def turn_3():
                    if old:
                        turn(u - 2, j, 3)

                def turn_4():
                    if old:
                        turn(u - 2, j, 4)

                def turn_0():
                    if new:
                        turn(u - 1, 1 - j, 0)

                if top < NU:
                    scores(u, j, 0, {2: turn_3, 3: turn_4})
                else:
                    turn_3()
                    turn_4()
                if old:
                    turn(u - 2, j, "o")
                    for g in (2, 3, 4):
                        times_v(u - 2, j, g)
                if top < NU:
                    scores(u, j, 1, {3: turn_0})
                else:
                    turn_0()
                if new:
                    turn(u - 1, 1 - j, 1)
                    turn(u - 1, 1 - j, 2)
                    times_v(u - 1, 1 - j, 0)
                    times_v(u - 1, 1 - j, 1)

            steps(e, body)
            turn(NU, 0, "o")

        def act_att(e):
            def leave(w, j, g):
                x = place(w, g)
                src = T_ps[bank(w, g)]
                if g == "o":
                    ge(e, s_ost[1 - j], 8 * (w - 2 + j))
                    e.wait_ge(s_T, x + 1)
                    e.activation(oT_s[:, 1 - j, :], src[:, 0, :], ACT.Copy).then_inc(s_Te, 1)
                    return
                ge(e, s_pv, NG * w + (-1, 0, -2, 1, 2)[g])
                e.wait_ge(s_T, x + 1)
                n = len(GROUPS[g])
                e.activation(probT[:, PT_SLOT[g], 0:n, :], src[:, 0:n, :], ACT.Copy).then_inc(s_Te, 1)

            def exps(u, j, m):
                if m == 0 and has(u, 2, NU):
                    e.wait_ge(s_T, place(u - 2, 4) + 1)
                if m == 1:
                    ge(e, s_comb, u)
                    ge(e, s_comb_p, u)
                e.wait_ge(s_nb, 2 * u + m + 1)
                dst = prob[:, j if m == 0 else 2, :]
                for c, (a, b) in enumerate(PARTS):
                    e.activation(dst[:, a:b], S_ps[:, a:b], ACT.Exp, bias=nbias[:, j, m:m + 1],
                                 accum_out=sums[:, j, m, c:c + 1]).then_inc(s_exp, 1)

            def body(u, j, top):
                if has(u, 1, NU + 1):
                    exps(u - 1, 1 - j, 1)
                if has(u, 2, NU + 2):
                    leave(u - 2, j, 3)
                    leave(u - 2, j, 4)
                    leave(u - 2, j, "o")
                if top < NU:
                    exps(u, j, 0)
                if has(u, 2, NU + 2):
                    e.wait_ge(s_o1, u - 1)
                    e.activation(o_sq1[:, :], o_s[:, j, :], ACT.Square, scale=P ** -0.5, accum_out=o_ss[:, j])\
                        .then_inc(s_osq, 1)
                if has(u, 1, NU + 1):
                    for g in range(3):
                        leave(u - 1, 1 - j, g)

            for c in range(K0_PARTS):
                cols = slice(c * K0, (c + 1) * K0)
                e.wait_ge(s_k0_in[c], 32)
                e.activation(k_hi[:, 0, :, cols], k0_raw[:, :, cols], ACT.Copy).then_inc(s_kh, LT // K0_PARTS)
            steps(e, body)
            leave(NU, 0, "o")

        def dve_att(e):
            e.memset(o_gated[:, 1, :], 0.0).then_inc(s_rv, 1)
            for c in range(K0_PARTS):
                cols = slice(c * K0, (c + 1) * K0)
                e.wait_ge(s_kh, LT // K0_PARTS * (c + 1))
                e.tensor_tensor(k_lo[:, 0, :, cols], k0_raw[:, :, cols], k_hi[:, 0, :, cols], ALU.subtract)\
                    .then_inc(s_ks, LT // K0_PARTS)

            def maxima(u, m, parts):
                for c in parts:
                    a, b = PARTS[c]
                    e.wait_ge(s_S, NPART * (2 * u + m) + c + 1)
                    e.tensor_reduce(amax[:, m, c:c + 1], S_ps[:, a:b], AX.X, ALU.max).then_inc(s_mx, 1)

            def bias(u, j, m):
                e.wait_ge(s_mx, NPART * (2 * u + m + 1))
                e.tensor_reduce(nbias[:, j, m:m + 1], amax[:, m, 0:NPART], AX.X, ALU.max, negate=True)\
                    .then_inc(s_nb, 1)

            def body(u, j, top):
                if top < NU:
                    maxima(u, 0, (0, 1, 2))
                    bias(u, j, 0)
                if has(u, 1, NU + 1):
                    e.wait_ge(s_c, 5 * u)
                    e.scalar_tensor_tensor(out=prob[:, 1 - j, 0:CUT], in0=prob[:, 2, 0:CUT], scalar=ratio[:, 1 - j, :],
                                           in1=prob[:, 1 - j, 0:CUT], op0=ALU.mult, op1=ALU.add).then_inc(s_comb, 1)
                if has(u, 2, NU + 2):
                    e.wait_ge(s_pv, NG * (u - 1))
                    e.tensor_scalar(o_s[:, j, :], O_ps, rden[:, j, 0:1], None, ALU.mult).then_inc(s_o1, 1)
                if top < NU:
                    maxima(u, 1, (0, 1, 2))
                    bias(u, j, 1)
                if has(u, 2, NU + 2):
                    e.wait_ge(s_g_in[j], 8 * (u - j))
                    ge(e, s_T, place(u - 3, "o") + 1)
                    e.wait_ge(s_ors, u - 1)
                    e.scalar_tensor_tensor(out=o_gated[:, j, :], in0=o_s[:, j, :], scalar=o_rstd[:, j],
                                           in1=g_in[:, j, :], op0=ALU.mult, op1=ALU.mult).then_inc(s_og, 1)

            steps(e, body)


        def sp_stored(e, p):
            for s in s_st:
                e.wait_ge(s, 8 * base(p, lambda r: not keeps_T(r)))
            if base(p, keeps_T):
                e.wait_ge(s_yst, 16 * base(p, keeps_T))

        @block.sync
        def _(e):
            sp_setup(e)
            stage_end(e, 1)
            for p in range(3):
                sp_pass(e, p)
            sp_stored(e, 3)
            stage_end(e, 2)
            sp_ret(e)
            stage_end(e, 3)
            for p in range(3, 8):
                sp_pass(e, p)
            sp_stored(e, 8)
            stage_end(e, 4)
            sp_att(e)
            stage_end(e, 5)
            sp_pass(e, 8)
            sp_stored(e, 9)

        @block.scalar
        def _(e):
            act_setup(e)
            stage_end(e, 1)
            for p in range(3):
                act_pass(e, p)
            stage_end(e, 2)
            act_ret(e)
            stage_end(e, 3)
            for p in range(3, 8):
                act_pass(e, p)
            stage_end(e, 4)
            act_att(e)
            stage_end(e, 5)
            act_pass(e, 8)

        @block.tensor
        def _(e):
            pe_setup(e)
            stage_end(e, 1)
            for p in range(3):
                pe_pass(e, p)
            stage_end(e, 2)
            pe_ret(e)
            stage_end(e, 3)
            for p in range(3, 8):
                pe_pass(e, p)
            stage_end(e, 4)
            pe_att(e)
            stage_end(e, 5)
            pe_pass(e, 8)

        @block.vector
        def _(e):
            dve_setup(e)
            stage_end(e, 1)
            for p in range(3):
                dve_pass(e, p)
            stage_end(e, 2)
            dve_ret(e)
            stage_end(e, 3)
            for p in range(3, 8):
                dve_pass(e, p)
            stage_end(e, 4)
            dve_att(e)
            stage_end(e, 5)
            dve_pass(e, 8)

        @block.gpsimd
        def _(e):
            pool_setup(e)
            stage_end(e, 1)
            for p in range(3):
                pool_pass(e, p)
            stage_end(e, 2)
            pool_ret(e)
            stage_end(e, 3)
            for p in range(3, 8):
                pool_pass(e, p)
            stage_end(e, 4)
            pool_att(e)
            stage_end(e, 5)
            pool_pass(e, 8)

_WEIGHTS = ["ada_w", "ada_b", "norm_post", "ev_w_in", "ev_w_out", "ret_decay_logit", "pool_w", "pool_scale",
            "od_w_in", "od_w_out", "diff_lambda", "diff_subln"]


def laid_out(inputs):
    a = {n: np.ascontiguousarray(inputs[n]) for n in _WEIGHTS}
    a["x_all"] = np.concatenate([np.asarray(inputs["ctx"])[0], np.asarray(inputs["x"])[0]])
    cond = np.stack([np.asarray(inputs["c_ctx"]), np.asarray(inputs["c"])[0]])
    a["cond"] = np.ascontiguousarray(cond.reshape(2, KC, P).transpose(2, 1, 0))
    a["npre"] = np.ascontiguousarray(np.asarray(inputs["norm_pre"]).reshape(2, KC, P).transpose(2, 0, 1))
    a["adab_cols"] = np.ascontiguousarray(np.asarray(inputs["ada_b"]).reshape(2, 3 * KC, P).transpose(2, 0, 1))
    a.update(host_constants())
    return a


def kernel(**inputs):
    from concourse import bacc
    from concourse.bass_utils import run_bass_kernel_spmd

    nc = bacc.Bacc("TRN2", target_bir_lowering=False, num_devices=1, dynamic_dma_scratch_size=1024)
    arrays = {f"in_{n}": a for n, a in laid_out(inputs).items()}
    aps = {n[3:]: nc.dram_tensor(n, a.shape, mybir.dt.from_np(a.dtype), kind="ExternalInput").ap()
           for n, a in arrays.items()}
    out = nc.dram_tensor("out_0", (1, SEQ, D), F32, kind="ExternalOutput").ap()
    build(nc, aps, out)
    r = run_bass_kernel_spmd(nc, [arrays], core_ids=[0])
    return r.results[0]["out_0"]
```
